# Optimizing a Trainium2 kernel written in Bass

```python
import jax
import jax.numpy as jnp
from jax import lax
import numpy as np

D_MODEL = 2048
BATCH = 1
SEQ = 256
DEPTH = 1

MIX_WIDTH = D_MODEL
RWKV_WIDTH = MIX_WIDTH // 2
RWKV_HEAD = 64
RWKV_HEADS = RWKV_WIDTH // RWKV_HEAD
DECAY_LORA = 64
AAA_LORA = 64
GATE_LORA = 160
RWKV_LN_EPS = 64e-5
ATT_WIDTH = MIX_WIDTH - RWKV_WIDTH
ATT_HEAD = 128
ATT_HEADS = ATT_WIDTH // ATT_HEAD
ATT_KV_HEADS = 2
IDX_HEADS = 16
IDX_HEAD = 64
TOPK_MAX = 256
Q_BLOCK = 128
ROPE_THETA = 500000.0
N_MEM = 256
CROSS_HEADS = 4
CROSS_HEAD = 128
D_FF = 4 * D_MODEL
NORM_EPS = 1e-5

RWKV_SPLITS = (RWKV_WIDTH, RWKV_WIDTH, RWKV_WIDTH, DECAY_LORA, AAA_LORA, GATE_LORA)
ATT_SPLITS = (ATT_WIDTH, ATT_KV_HEADS * ATT_HEAD, ATT_KV_HEADS * ATT_HEAD,
              IDX_HEADS * IDX_HEAD, IDX_HEAD, IDX_HEADS)
RWKV_COLS = sum(RWKV_SPLITS)
ATT_COLS = sum(ATT_SPLITS)
IN_COLS = RWKV_COLS + ATT_COLS


def split_cols(t, sizes):
    out, start = [], 0
    for s in sizes:
        out.append(t[..., start:start + s])
        start += s
    return out

def rms_norm(x, g):
    xf = x.astype(jnp.float32)
    y = xf * lax.rsqrt(jnp.mean(xf * xf, axis=-1, keepdims=True) + NORM_EPS)
    return (y * g.astype(jnp.float32)).astype(x.dtype)

def partial_rope(x, pos):
    dh = x.shape[-1]
    rot = dh // 4
    half = rot // 2
    inv_freq = ROPE_THETA ** (-jnp.arange(half, dtype=jnp.float32) / half)
    ang = pos.astype(jnp.float32)[..., None] * inv_freq
    cos = jnp.cos(ang)[:, :, None, :]
    sin = jnp.sin(ang)[:, :, None, :]
    xr = x[..., :rot].astype(jnp.float32)
    x1, x2 = xr[..., :half], xr[..., half:]
    rotated = jnp.concatenate([x1 * cos - x2 * sin, x2 * cos + x1 * sin], axis=-1).astype(x.dtype)
    return jnp.concatenate([rotated, x[..., rot:]], axis=-1)

def rwkv7_group(p, mu, w0, w_decay_up, a0, a_up, g_up, k_k, k_a, r_k, lnx_w, lnx_b):
    B, S, _ = p.shape
    H, N = RWKV_HEADS, RWKV_HEAD
    f32 = jnp.float32
    prev = jnp.pad(p, ((0, 0), (1, 0), (0, 0)))[:, :-1]
    p = p + (prev - p) * mu
    r, k, v, xw, xa, xg = split_cols(p, RWKV_SPLITS)
    w = -jax.nn.softplus(-(w0 + jnp.tanh(xw) @ w_decay_up)) - 0.5
    decay = jnp.exp(-jnp.exp(w.astype(f32)))
    a = jax.nn.sigmoid(a0 + xa @ a_up)
    g = jax.nn.sigmoid(xg) @ g_up
    heads = lambda t: t.astype(f32).reshape(B, S, H, N)
    kk = heads(k * k_k)
    kk = kk / jnp.maximum(jnp.sqrt(jnp.sum(kk * kk, axis=-1, keepdims=True)), 1e-12)
    k = k * (1.0 + (a - 1.0) * k_a)
    r4, k4, v4, a4, w4 = heads(r), heads(k), heads(v), heads(a), decay.reshape(B, S, H, N)

    def step(state, inp):
        r_t, w_t, k_t, v_t, kk_t, a_t = inp
        sa = jnp.einsum('bhvk,bhk->bhv', state, -kk_t)
        state = (state * w_t[:, :, None, :]
                 + sa[..., None] * (kk_t * a_t)[:, :, None, :]
                 + v_t[..., None] * k_t[:, :, None, :])
        return state, jnp.einsum('bhvk,bhk->bhv', state, r_t)

    tm = lambda t: jnp.swapaxes(t, 0, 1)
    s0 = jnp.zeros((B, H, N, N), f32)
    _, y = lax.scan(step, s0, (tm(r4), tm(w4), tm(k4), tm(v4), tm(kk), tm(a4)))
    y = tm(y)
    mean = jnp.mean(y, axis=-1, keepdims=True)
    var = jnp.mean(jnp.square(y - mean), axis=-1, keepdims=True)
    yn = ((y - mean) * lax.rsqrt(var + RWKV_LN_EPS)).reshape(B, S, RWKV_WIDTH)
    yn = yn * lnx_w.astype(f32) + lnx_b.astype(f32)
    bonus = (jnp.sum(r4 * k4 * r_k.astype(f32), axis=-1, keepdims=True) * v4).reshape(B, S, RWKV_WIDTH)
    return ((yn + bonus) * g.astype(f32)).astype(p.dtype)

def dsa_group(p, pos):
    B, S, _ = p.shape
    f32 = jnp.float32
    G = ATT_HEADS // ATT_KV_HEADS
    q, k, v, qi, ki, wi = split_cols(p, ATT_SPLITS)
    q = partial_rope(q.reshape(B, S, ATT_HEADS, ATT_HEAD), pos)
    k = partial_rope(k.reshape(B, S, ATT_KV_HEADS, ATT_HEAD), pos)
    v = v.reshape(B, S, ATT_KV_HEADS, ATT_HEAD)
    qi = partial_rope(qi.reshape(B, S, IDX_HEADS, IDX_HEAD), pos)
    ki = partial_rope(ki.reshape(B, S, 1, IDX_HEAD), pos)[:, :, 0].astype(f32)
    wi = wi.astype(f32) * (IDX_HEADS ** -0.5 * IDX_HEAD ** -0.5)
    n_sel = min(TOPK_MAX, S // 4)
    nblk = S // Q_BLOCK
    key_pos = jnp.arange(S)
    gather = jax.vmap(lambda t, i: t[i])

    def to_blocks(t):
        return jnp.swapaxes(t.reshape((B, nblk, Q_BLOCK) + t.shape[2:]), 0, 1)

    def block(args):
        bi, qb, qib, wib = args
        q_pos = bi * Q_BLOCK + jnp.arange(Q_BLOCK)
        rel = jax.nn.relu(jnp.einsum('bqhd,bsd->bqhs', qib.astype(f32), ki))
        score = jnp.einsum('bqhs,bqh->bqs', rel, wib)
        causal = key_pos[None, :] <= q_pos[:, None]
        score = jnp.where(causal[None], score, -1e30)
        _, idx = lax.top_k(score, n_sel)
        valid = idx <= q_pos[None, :, None]
        kg = gather(k, idx)
        vg = gather(v, idx)
        qg = qb.reshape(B, Q_BLOCK, ATT_KV_HEADS, G, ATT_HEAD)
        s = jnp.einsum('bqhgd,bqkhd->bqhgk', qg, kg).astype(f32) * (ATT_HEAD ** -0.5)
        s = jnp.where(valid[:, :, None, None, :], s, -jnp.inf)
        prob = jax.nn.softmax(s, axis=-1).astype(vg.dtype)
        o = jnp.einsum('bqhgk,bqkhd->bqhgd', prob, vg)
        return o.reshape(B, Q_BLOCK, ATT_WIDTH)

    out = lax.map(block, (jnp.arange(nblk), to_blocks(q), to_blocks(qi), to_blocks(wi)))
    return jnp.swapaxes(out, 0, 1).reshape(B, S, ATT_WIDTH)

def memory_cross_attention(hn, mem_n, w_q, w_kv, w_o):
    B, S, _ = hn.shape
    M = mem_n.shape[1]
    q = (hn @ w_q).reshape(B, S, CROSS_HEADS, CROSS_HEAD)
    k, v = split_cols(mem_n @ w_kv, (CROSS_HEADS * CROSS_HEAD, CROSS_HEADS * CROSS_HEAD))
    k = k.reshape(B, M, CROSS_HEADS, CROSS_HEAD)
    v = v.reshape(B, M, CROSS_HEADS, CROSS_HEAD)
    s = jnp.einsum('bshd,bmhd->bhsm', q, k).astype(jnp.float32) * (CROSS_HEAD ** -0.5)
    prob = jax.nn.softmax(s, axis=-1).astype(v.dtype)
    o = jnp.einsum('bhsm,bmhd->bshd', prob, v).reshape(B, S, CROSS_HEADS * CROSS_HEAD)
    return o @ w_o

def first_inputs(seed: int = 0) -> dict:
    key = jax.random.key(seed)
    ks = jax.random.split(key, 32)
    f32 = jnp.float32
    L = DEPTH

    def dense(k, fan_in, shape):
        return jax.random.normal(k, shape, f32) * fan_in ** -0.5

    def gain(k, shape):
        return 1.0 + 0.02 * jax.random.normal(k, shape, f32)

    return {
        'x': jax.random.normal(ks[0], (BATCH, SEQ, D_MODEL), f32),
        'mem': jax.random.normal(ks[1], (BATCH, N_MEM, D_MODEL), f32),
        'positions': jnp.tile(jnp.arange(SEQ, dtype=jnp.int32)[None, :], (BATCH, 1)),
        'norm_mix': gain(ks[2], (L, D_MODEL)),
        'w_in': dense(ks[3], D_MODEL, (L, D_MODEL, IN_COLS)),
        'rwkv_mu': jax.random.uniform(ks[4], (L, RWKV_COLS), f32),
        'w_decay0': jax.random.uniform(ks[5], (L, RWKV_WIDTH), f32, -6.0, 1.0),
        'w_decay_up': dense(ks[6], DECAY_LORA, (L, DECAY_LORA, RWKV_WIDTH)),
        'a0': 0.1 * jax.random.normal(ks[7], (L, RWKV_WIDTH), f32),
        'a_up': dense(ks[8], AAA_LORA, (L, AAA_LORA, RWKV_WIDTH)),
        'g_up': dense(ks[9], GATE_LORA, (L, GATE_LORA, RWKV_WIDTH)),
        'k_k': 0.85 + 0.05 * jax.random.normal(ks[10], (L, RWKV_WIDTH), f32),
        'k_a': 1.0 + 0.05 * jax.random.normal(ks[11], (L, RWKV_WIDTH), f32),
        'r_k': 0.1 * jax.random.normal(ks[12], (L, RWKV_HEADS, RWKV_HEAD), f32),
        'lnx_w': gain(ks[13], (L, RWKV_WIDTH)),
        'lnx_b': 0.02 * jax.random.normal(ks[14], (L, RWKV_WIDTH), f32),
        'w_mix_out': dense(ks[15], MIX_WIDTH, (L, MIX_WIDTH, D_MODEL)),
        'norm_cross': gain(ks[16], (L, D_MODEL)),
        'norm_mem': gain(ks[17], (L, D_MODEL)),
        'w_q_cross': dense(ks[18], D_MODEL, (L, D_MODEL, CROSS_HEADS * CROSS_HEAD)),
        'w_kv_cross': dense(ks[19], D_MODEL, (L, D_MODEL, 2 * CROSS_HEADS * CROSS_HEAD)),
        'w_o_cross': dense(ks[20], CROSS_HEADS * CROSS_HEAD, (L, CROSS_HEADS * CROSS_HEAD, D_MODEL)),
        'norm_mlp': gain(ks[21], (L, D_MODEL)),
        'w_up': dense(ks[22], D_MODEL, (L, D_MODEL, D_FF)),
        'w_down': dense(ks[23], D_FF, (L, D_FF, D_MODEL)),
        'norm_final': gain(ks[24], (D_MODEL,)),
    }

def first_block(x, mem, positions, norm_mix, w_in, rwkv_mu, w_decay0, w_decay_up, a0, a_up, g_up,
              k_k, k_a, r_k, lnx_w, lnx_b, w_mix_out, norm_cross, norm_mem, w_q_cross,
              w_kv_cross, w_o_cross, norm_mlp, w_up, w_down, norm_final):
    h = x
    for l in range(DEPTH):
        p = rms_norm(h, norm_mix[l]) @ w_in[l]
        y_rwkv = rwkv7_group(p[..., :RWKV_COLS], rwkv_mu[l], w_decay0[l], w_decay_up[l], a0[l],
                             a_up[l], g_up[l], k_k[l], k_a[l], r_k[l], lnx_w[l], lnx_b[l])
        y_att = dsa_group(p[..., RWKV_COLS:], positions)
        h = h + jnp.concatenate([y_rwkv, y_att], axis=-1) @ w_mix_out[l]
        h = h + memory_cross_attention(rms_norm(h, norm_cross[l]), rms_norm(mem, norm_mem[l]),
                                       w_q_cross[l], w_kv_cross[l], w_o_cross[l])
        u = rms_norm(h, norm_mlp[l]) @ w_up[l]
        h = h + jnp.square(jax.nn.relu(u)) @ w_down[l]
    return rms_norm(h, norm_final)


GRID_W = 64
CTX_LEN = 256
N_MIXERS = 3
N_MOD = 6
EPS = 1e-6
NEG_INF = -1e30
D_FF_2 = 5632
FFN_CONV = 3
CHUNK = 128
A_WIDTH = 2 * D_MODEL
A_GROUPS = 16
NA_HEADS = 16
NA_HEAD_DIM = D_MODEL // NA_HEADS
NA_KH_MAX = 8
NA_KW = 16
RNN_WIDTH = D_MODEL
RNN_HEADS = 16
RNN_HEAD_DIM = RNN_WIDTH // RNN_HEADS
RNN_CONV = 4
RG_C = 8.0
N_A_LAYERS = (DEPTH + N_MIXERS - 1) // N_MIXERS
N_B_LAYERS = (DEPTH + N_MIXERS - 2) // N_MIXERS
N_C_LAYERS = (DEPTH + N_MIXERS - 3) // N_MIXERS


def rmsnorm(x, g):
    xf = x.astype(jnp.float32)
    y = xf * lax.rsqrt(jnp.mean(xf * xf, axis=-1, keepdims=True) + EPS)
    return (y * g.astype(jnp.float32)).astype(x.dtype)

def modulate(h, shift, scale):
    return h * (1 + scale) + shift

def dwconv(x, w, b, left):
    k, length = w.shape[0], x.shape[1]
    xp = jnp.pad(x, ((0, 0), (left, k - 1 - left), (0, 0)))
    y = b
    for j in range(k):
        y = y + xp[:, j:j + length] * w[j]
    return y

def conv_ffn(h, w_up, conv_w, conv_b, w_down):
    z = dwconv(h @ w_up, conv_w, conv_b, FFN_CONV // 2)
    g, v = jnp.split(z, 2, axis=-1)
    return (jax.nn.silu(g) * v) @ w_down

def chunk_mlp_mix(h, w_in, g_v, w_s, b_s, w_out):
    bsz, length, _ = h.shape
    z = jax.nn.gelu(h @ w_in)
    u, v = jnp.split(z, 2, axis=-1)
    v = rmsnorm(v, g_v).reshape(bsz, length // CHUNK, CHUNK, A_GROUPS, A_WIDTH // A_GROUPS)
    s = jnp.einsum('gpq,bnqgc->bnpgc', w_s, v) + b_s.T[None, None, :, :, None]
    return (u * s.reshape(bsz, length, A_WIDTH)) @ w_out

def na_mix(hc, hl, w_qkv, rpb, w_out, need_ctx):
    bsz, seq, _ = hl.shape
    rows = seq // GRID_W
    kh = min(NA_KH_MAX, rows)
    scale = NA_HEAD_DIM ** -0.5
    qkv = (hl @ w_qkv).reshape(bsz, rows, GRID_W, 3, NA_HEADS, NA_HEAD_DIM)
    q, k, v = qkv[:, :, :, 0], qkv[:, :, :, 1], qkv[:, :, :, 2]
    if need_ctx:
        qkv_c = (hc @ w_qkv).reshape(bsz, hc.shape[1], 3, NA_HEADS, NA_HEAD_DIM)
        q_c, k_c, v_c = qkv_c[:, :, 0], qkv_c[:, :, 1], qkv_c[:, :, 2]
    else:
        kv_c = (hc @ w_qkv[:, D_MODEL:]).reshape(bsz, hc.shape[1], 2, NA_HEADS, NA_HEAD_DIM)
        k_c, v_c = kv_c[:, :, 0], kv_c[:, :, 1]
    r = jnp.arange(rows)
    r0 = jnp.clip(r - kh // 2, 0, rows - kh)
    key_rows = r0[:, None] + jnp.arange(kh)[None, :]
    col = jnp.arange(GRID_W)
    c0 = jnp.clip(col - NA_KW // 2, 0, GRID_W - NA_KW)
    col_ok = (col[None, :] >= c0[:, None]) & (col[None, :] < c0[:, None] + NA_KW)
    k_blk = k[:, key_rows]
    v_blk = v[:, key_rows]
    s_lat = jnp.einsum('brqhd,brikhd->bhrqik', q, k_blk).astype(jnp.float32) * scale
    dr = key_rows - r[:, None]
    dc = jnp.clip(col[None, :] - col[:, None], -(NA_KW - 1), NA_KW - 1)
    bias = rpb[:, dr[:, None, :, None] + NA_KH_MAX - 1, dc[None, :, None, :] + NA_KW - 1]
    s_lat = jnp.where(col_ok[None, None, None, :, None, :], s_lat + bias[None].astype(jnp.float32), NEG_INF)
    s_ctx = jnp.einsum('brqhd,bkhd->bhrqk', q, k_c).astype(jnp.float32) * scale
    n_win = kh * GRID_W
    logits = jnp.concatenate([s_lat.reshape(bsz, NA_HEADS, rows, GRID_W, n_win), s_ctx], axis=-1)
    p = jax.nn.softmax(logits, axis=-1).astype(v.dtype)
    p_lat = p[..., :n_win].reshape(bsz, NA_HEADS, rows, GRID_W, kh, GRID_W)
    o = jnp.einsum('bhrqik,brikhd->brqhd', p_lat, v_blk) + jnp.einsum('bhrqk,bkhd->brqhd', p[..., n_win:], v_c)
    y_lat = o.reshape(bsz, seq, D_MODEL) @ w_out
    y_ctx = None
    if need_ctx:
        sc = jnp.einsum('bqhd,bkhd->bhqk', q_c, k_c).astype(jnp.float32) * scale
        pc = jax.nn.softmax(sc, axis=-1).astype(v_c.dtype)
        y_ctx = jnp.einsum('bhqk,bkhd->bqhd', pc, v_c).reshape(bsz, hc.shape[1], D_MODEL) @ w_out
    return y_ctx, y_lat

def rglru_gates(xr, w_g, b_g, lam):
    bsz, length, _ = xr.shape
    xh = xr.reshape(bsz, length, RNN_HEADS, RNN_HEAD_DIM)
    g = jnp.einsum('blhi,ghij->gblhj', xh, w_g) + b_g[:, None, None]
    g = jax.nn.sigmoid(g.astype(jnp.float32)).reshape(2, bsz, length, RNN_WIDTH)
    log_a = -RG_C * g[0] * jax.nn.softplus(-lam.astype(jnp.float32))
    a = jnp.exp(log_a)
    b = jnp.sqrt(-jnp.expm1(2.0 * log_a)) * (g[1] * xr.astype(jnp.float32))
    return a, b

def linear_scan(a, b, h0, reverse):
    idx = -1 if reverse else 0
    b = b.at[:, idx].add(a[:, idx] * h0)

    def combine(e1, e2):
        a1, b1 = e1
        a2, b2 = e2
        return a1 * a2, a2 * b1 + b2

    _, h = lax.associative_scan(combine, (a, b), reverse=reverse, axis=1)
    return h

def rglru_mix(hc, hl, w_in, conv_w, conv_b, w_gate, b_gate, lam, w_out, need_ctx):
    left = RNN_CONV // 2
    if need_ctx:
        y_c, x_c = jnp.split(hc @ w_in, 2, axis=-1)
    else:
        x_c = hc @ w_in[:, RNN_WIDTH:]
    x_c = dwconv(x_c, conv_w, conv_b, left)
    y_l, x_l = jnp.split(hl @ w_in, 2, axis=-1)
    x_l = dwconv(x_l, conv_w, conv_b, left)
    h0 = jnp.zeros((hc.shape[0], RNN_WIDTH), jnp.float32)
    h_c_dirs, h_l_dirs = [], []
    for d, rev in enumerate((False, True)):
        a_c, b_c = rglru_gates(x_c, w_gate[d], b_gate[d], lam[d])
        h_c = linear_scan(a_c, b_c, h0, rev)
        h_end = h_c[:, 0] if rev else h_c[:, -1]
        a_l, b_l = rglru_gates(x_l, w_gate[d], b_gate[d], lam[d])
        h_l_dirs.append(linear_scan(a_l, b_l, h_end, rev))
        h_c_dirs.append(h_c)
    h_l = (h_l_dirs[0] + h_l_dirs[1]).astype(hl.dtype)
    y_lat = (jax.nn.gelu(y_l) * h_l) @ w_out
    y_ctx = None
    if need_ctx:
        h_cs = (h_c_dirs[0] + h_c_dirs[1]).astype(hc.dtype)
        y_ctx = (jax.nn.gelu(y_c) * h_cs) @ w_out
    return y_ctx, y_lat

def second_inputs(seed: int = 0) -> dict:
    key = jax.random.key(seed)
    ks = iter(jax.random.split(key, 32))

    def nrm(shape, scale):
        return jax.random.normal(next(ks), shape, jnp.float32) * scale

    D = D_MODEL
    nA, nB, nC = N_A_LAYERS, N_B_LAYERS, N_C_LAYERS
    a0 = jax.random.uniform(next(ks), (nC, 2, RNN_WIDTH), jnp.float32, 0.9, 0.999)
    s = a0 ** (1.0 / RG_C)
    c_lam = jnp.log(s) - jnp.log1p(-s)
    return {
        'x': nrm((BATCH, SEQ, D), 1.0),
        'c': nrm((BATCH, D), 1.0),
        'ctx': nrm((BATCH, CTX_LEN, D), 1.0),
        'c_ctx': nrm((D,), 1.0),
        'ada_w': nrm((DEPTH, D, N_MOD * D), D ** -0.5),
        'ada_b': nrm((DEPTH, N_MOD * D), 0.02),
        'norm_g': 1.0 + nrm((DEPTH, 2, D), 0.05),
        'ffn_w_up': nrm((DEPTH, D, 2 * D_FF_2), D ** -0.5),
        'ffn_conv_w': nrm((DEPTH, FFN_CONV, 2 * D_FF_2), FFN_CONV ** -0.5),
        'ffn_conv_b': nrm((DEPTH, 2 * D_FF_2), 0.02),
        'ffn_w_down': nrm((DEPTH, D_FF_2, D), D_FF_2 ** -0.5),
        'a_w_in': nrm((nA, D, 2 * A_WIDTH), D ** -0.5),
        'a_g_v': 1.0 + nrm((nA, A_WIDTH), 0.05),
        'a_w_s': nrm((nA, A_GROUPS, CHUNK, CHUNK), CHUNK ** -0.5),
        'a_b_s': nrm((nA, A_GROUPS, CHUNK), 0.1),
        'a_w_out': nrm((nA, A_WIDTH, D), A_WIDTH ** -0.5),
        'b_w_qkv': nrm((nB, D, 3 * D), D ** -0.5),
        'b_rpb': nrm((nB, NA_HEADS, 2 * NA_KH_MAX - 1, 2 * NA_KW - 1), 0.2),
        'b_w_out': nrm((nB, D, D), D ** -0.5),
        'c_w_in': nrm((nC, D, 2 * RNN_WIDTH), D ** -0.5),
        'c_conv_w': nrm((nC, RNN_CONV, RNN_WIDTH), RNN_CONV ** -0.5),
        'c_conv_b': nrm((nC, RNN_WIDTH), 0.02),
        'c_w_gate': nrm((nC, 2, 2, RNN_HEADS, RNN_HEAD_DIM, RNN_HEAD_DIM), RNN_HEAD_DIM ** -0.5),
        'c_b_gate': nrm((nC, 2, 2, RNN_HEADS, RNN_HEAD_DIM), 0.1),
        'c_lam': c_lam,
        'c_w_out': nrm((nC, RNN_WIDTH, D), RNN_WIDTH ** -0.5),
        'final_g': 1.0 + nrm((D,), 0.05),
    }

def second_block(x, c, ctx, c_ctx, ada_w, ada_b, norm_g, ffn_w_up, ffn_conv_w, ffn_conv_b, ffn_w_down,
              a_w_in, a_g_v, a_w_s, a_b_s, a_w_out, b_w_qkv, b_rpb, b_w_out,
              c_w_in, c_conv_w, c_conv_b, c_w_gate, c_b_gate, c_lam, c_w_out, final_g):
    bsz = x.shape[0]
    silu_c = jax.nn.silu(c)
    silu_cc = jax.nn.silu(c_ctx)
    h_lat, h_ctx = x, ctx
    for i in range(DEPTH):
        last = i == DEPTH - 1
        kind, j = i % N_MIXERS, i // N_MIXERS
        ctx_in = (not last) or kind != 0
        m_l = (silu_c @ ada_w[i] + ada_b[i]).reshape(bsz, 1, N_MOD, D_MODEL)
        n_l = modulate(rmsnorm(h_lat, norm_g[i, 0]), m_l[:, :, 0], m_l[:, :, 1])
        if ctx_in:
            m_c = (silu_cc @ ada_w[i] + ada_b[i]).reshape(N_MOD, D_MODEL)
            n_c = modulate(rmsnorm(h_ctx, norm_g[i, 0]), m_c[0], m_c[1])
        if kind == 0:
            y_l = chunk_mlp_mix(n_l, a_w_in[j], a_g_v[j], a_w_s[j], a_b_s[j], a_w_out[j])
            y_c = None if last else chunk_mlp_mix(n_c, a_w_in[j], a_g_v[j], a_w_s[j], a_b_s[j], a_w_out[j])
        elif kind == 1:
            y_c, y_l = na_mix(n_c, n_l, b_w_qkv[j], b_rpb[j], b_w_out[j], not last)
        else:
            y_c, y_l = rglru_mix(n_c, n_l, c_w_in[j], c_conv_w[j], c_conv_b[j], c_w_gate[j], c_b_gate[j],
                                 c_lam[j], c_w_out[j], not last)
        h_lat = h_lat + m_l[:, :, 2] * y_l
        n_l = modulate(rmsnorm(h_lat, norm_g[i, 1]), m_l[:, :, 3], m_l[:, :, 4])
        h_lat = h_lat + m_l[:, :, 5] * conv_ffn(n_l, ffn_w_up[i], ffn_conv_w[i], ffn_conv_b[i], ffn_w_down[i])
        if not last:
            h_ctx = h_ctx + m_c[2] * y_c
            n_c = modulate(rmsnorm(h_ctx, norm_g[i, 1]), m_c[3], m_c[4])
            h_ctx = h_ctx + m_c[5] * conv_ffn(n_c, ffn_w_up[i], ffn_conv_w[i], ffn_conv_b[i], ffn_w_down[i])
    return rmsnorm(h_lat, final_g)


def setup_inputs(seed=0):
    out = dict(first_inputs(seed))
    for name, value in second_inputs(seed + 1).items():
        if name != "x":
            out[name + "_2"] = value
    return out


def reference(
    x, mem, positions, norm_mix, w_in, rwkv_mu, w_decay0, w_decay_up, a0, a_up, g_up, k_k, k_a,
    r_k, lnx_w, lnx_b, w_mix_out, norm_cross, norm_mem, w_q_cross, w_kv_cross, w_o_cross,
    norm_mlp, w_up, w_down, norm_final, c_2, ctx_2, c_ctx_2, ada_w_2, ada_b_2, norm_g_2,
    ffn_w_up_2, ffn_conv_w_2, ffn_conv_b_2, ffn_w_down_2, a_w_in_2, a_g_v_2, a_w_s_2, a_b_s_2,
    a_w_out_2, b_w_qkv_2, b_rpb_2, b_w_out_2, c_w_in_2, c_conv_w_2, c_conv_b_2, c_w_gate_2,
    c_b_gate_2, c_lam_2, c_w_out_2, final_g_2,
):
    x = first_block(
        x, mem, positions, norm_mix, w_in, rwkv_mu, w_decay0, w_decay_up, a0, a_up, g_up, k_k,
        k_a, r_k, lnx_w, lnx_b, w_mix_out, norm_cross, norm_mem, w_q_cross, w_kv_cross,
        w_o_cross, norm_mlp, w_up, w_down, norm_final,
    )
    return second_block(
        x, c_2, ctx_2, c_ctx_2, ada_w_2, ada_b_2, norm_g_2, ffn_w_up_2, ffn_conv_w_2,
        ffn_conv_b_2, ffn_w_down_2, a_w_in_2, a_g_v_2, a_w_s_2, a_b_s_2, a_w_out_2, b_w_qkv_2,
        b_rpb_2, b_w_out_2, c_w_in_2, c_conv_w_2, c_conv_b_2, c_w_gate_2, c_b_gate_2, c_lam_2,
        c_w_out_2, final_g_2,
    )


_drawn_inputs = setup_inputs


def setup_inputs(seed=0):
    import zlib

    import numpy as np

    out = dict(_drawn_inputs(seed))
    spreads = {}
    factors = {'a0': 3.11,
     'k_k': 3.615,
     'lnx_w': 5.928,
     'lnx_b': 6.297,
     'norm_cross': 8.0,
     'norm_mem': 8.0,
     'norm_mlp': 7.546,
     'ffn_conv_b_2': 5.219}
    for name, (base, spread) in spreads.items():
        noise = np.random.default_rng([zlib.crc32(name.encode()), seed]).standard_normal(out[name].shape)
        drawn = base * np.exp(spread * noise) if base else spread * noise
        out[name] = jnp.asarray(drawn.astype(out[name].dtype))
    for name, factor in factors.items():
        out[name] = (out[name] * factor).astype(out[name].dtype)
    return out
```

```python
from contextlib import ExitStack

import numpy as np

import concourse.bass as bass
from concourse import mybir

F32 = mybir.dt.float32
F32R = mybir.dt.float32r
I32 = mybir.dt.int32
U8 = mybir.dt.uint8
ALU = mybir.AluOpType
ACT = mybir.ActivationFunctionType
AX_X = mybir.AxisListType.X

P = 128
T = 256
D = 2048
DC = D // P
HEAD = 64
RW = 1024
RWT = RW // P
CH = 64
FF2 = 5632
FF2C = FF2 // P
AWC = 4096 // P
RING = 4
SLOT = 1024
EPS_1 = 1e-5
EPS_2 = 1e-6
EPS_HEAD = 64e-5
THETA = 500000.0
ATT_SCALE = 128 ** -0.5
IDX_SCALE = 16 ** -0.5 * 64 ** -0.5
N_SEL = 64

W_IN = [8] * 12
MIX_OUT = [8] * 4
KV_CROSS = [8] * 2
Q_CROSS = [8]
O_CROSS = [2] * 4
MLP = [8] * 8
A_V = [8] * 8
A_UO = [8] * 8
FFN = [8] * 12
FFN_TAIL = [8] * 6 + [6] * 4

COL = {}
_n = 0
for _name, _w in [("spare", 24), ("norm_mix", DC), ("norm_cross", DC), ("norm_mem", DC), ("norm_mlp", DC), ("norm_final", DC),
                  ("norm_g0", DC), ("norm_g1", DC), ("final_g", DC), ("c", DC), ("ada_b", 96), ("g_v", AWC),
                  ("conv", FF2C * 8), ("mu", 27), ("w0", RWT), ("a0", RWT), ("k_k", RWT), ("k_a", RWT),
                  ("r_k", RWT), ("lnx_w", RWT), ("lnx_b", RWT), ("inv_freq", 2), ("i64", CH)]:
    COL[_name] = _n
    _n += _w
NPAR = _n

T_R, T_K, T_V, T_Q, T_KA, T_VA, T_QI, T_LORA, T_KI = 0, 8, 16, 24, 32, 34, 36, 44, 47
NT = 48
TW = T + 1

C_ID, C_ONES, C_BLK1, C_BLK64, C_ROPE, C_ROPEI, C_DUP, C_DUPR = range(8)


class Steps:

    def __init__(self, sems, names):
        self.sems, self.names, self.next = sems, names.split(), [0] * len(sems)

    def wait(self, eng, g, i, name):
        eng.wait_ge(self.sems[g], len(self.names) * i + self.names.index(name) + 1)

    def done(self, ins, g, name):
        assert self.names[self.next[g]] == name, (self.names[self.next[g]], name)
        self.next[g] = (self.next[g] + 1) % len(self.names)
        ins.then_inc(self.sems[g], 1)


def make_mixers(nc, at, sem, A, K, e):
    proj, par, col, one, ps, ident, act_in = (e[x] for x in "proj par col one ps ident act_in".split())
    apart = e["apart"]
    O1, O2, O3 = e["O_HI"], e["O_ACT"] + 16 * K, e["O_KV"]
    lanes = range(2)

    def lane(name, shape, off, stride):
        return [at(f"{name}{g}", shape, off + g * stride) for g in lanes]

    W = 32 * K
    rkv = lane("rkv", [P, 3, T], O1, W)
    ar = lane("ar", [P, 2, T], O1 + 3 * K, W)
    bk = lane("bk", [P, 2, T], O1 + 5 * K, W)
    dec = lane("dec", [P, 3, T], O1 + 7 * K, W)
    lda = lane("lda", [P, 2, T], O1 + 10 * K, W)
    cs = lane("cs", [P, T], O1 + 12 * K, W)
    kk = lane("kk", [P, T], O1 + 13 * K, W)
    tm = lane("tm", [P, 4, 2, P], O1 + 14 * K, W)
    lm = lane("lm", [P, 4, 4, P], O1 + 18 * K, W)
    tmp = lane("tmp", [P, 8, T], O1 + 18 * K, W)
    bt = lane("bt", [P, 4, P], O1 + 26 * K, W)
    pp = lane("pp", [P, 4, P], O1 + 28 * K, W)
    mt = lane("mt", [P, 2, CH], O1 + 30 * K, W)
    nn = lane("nn", [P, 3, CH], O1 + 30 * K + 512, W)
    st = lane("st", [P, 2, CH], O1 + 31 * K + 256, W)
    xx = lane("xx", [P, 4, P], O2, 4 * K)
    xt = lane("xt", [P, 4, P], O2 + 2 * K, 4 * K)
    r2 = lane("r2", [P, T], O2 + 8 * K, 4 * K)
    y1 = lane("y1", [P, T], O2 + 9 * K, 4 * K)
    gg = lane("gg", [P, T], O2 + 10 * K, 4 * K)
    bo = lane("bo", [P, T], O2 + 11 * K, 4 * K)
    lw = lane("lw", [P, 4, P], O3, 2 * K)
    lx = at("lx", [P, 3, T], O3 + 4 * K)
    mk = at("mk", [P, 12, P], O3 + 7 * K)
    blk = at("blk", [P, 2, P], O3 + 13 * K)
    rn = lane("rn", [P, T], O3 + 14 * K, K)
    i64 = par[:, COL["i64"]:COL["i64"] + CH]
    omka = par[:, COL["spare"] + 16:COL["spare"] + 16 + RWT]
    tab = at("tab", [P, 4, T], e["O_HL"])
    tp = at("tp", [P, 3, T], e["O_HL"] + 4 * K)
    posi = at("posi", [P, T], e["O_HL"] + 7 * K, I32)
    cm = at("cm", [P, 4, P], O1)
    ki2 = at("ki2", [P, T], O1 + 2 * K)
    wi = at("wi", [P, 2, 16], O1 + 3 * K)
    sc = at("sc", [P, 384], O1 + 4 * K)
    wk = at("wk", [P, 384], O1 + 6 * K)
    bias = at("bias", [P, 384], O1 + 8 * K)
    m8 = at("m8", [P, 2, 8], O1 + 10 * K)
    qs = lane("qs", [P, T], O1 + 12 * K, K)
    rt = lane("rt", [P, 2, T], O1 + 14 * K, 2 * K)
    rel = lane("rel", [P, 2, 384], O1 + 18 * K, 3 * K)
    vf = at("vf", [P, T], O1 + 24 * K)
    vs = at("vs", [P, 2, P], O1 + 25 * K)
    sm = lane("sm", [P, 384], O1 + 26 * K, 2 * K)
    pt = lane("pt", [P, 3, P], O1 + 30 * K, 2 * K)
    sx_ = at("sx_", [P, 4, 4], O1 + 34 * K)

    def steps(name, names):
        return Steps([sem(f"{name}{g}") for g in lanes], names)

    RD = steps("rwkv_d", "r0 r k0 k v0 v kr kq ld cs cp km kv kk am k2 bp bo at rt b0 bt kt tb l0 l1 l2 l3 m0 x0 xt0 "
                         "m1 m2 xt1 x1 m3 xt2 x2 m4 xt3 x3 m5 xt4 x4 xt5 zw r2 mt1 mt2 n0 n1 n2 s2a s2b s3a s3b "
                         "ya yb yc yq ve vi yn yw yo yg lo")
    RA = steps("rwkv_a", "sg aa gg e1 e2 e3 root ta c1 c2 c3 c4 c5 za ac y1 vr hi")
    RT = steps("rwkv_t", "lora kn bs tr ll p0 p1 q1 p2 q2 p3 q3 p4 q4 p5 q5 w au ry mn s1 s2 yy mu va")
    lw_in = [sem("lw_in0"), sem("lw_in1")]
    mk_in, cm_in, pos_in = sem("mk_in"), sem("cm_in"), sem("pos_in")
    pre_d, pre_a, tab_p = sem("pre_d"), sem("pre_a"), sem("tab_p")
    ID = steps("index_d", "t u q a0 a1 a2 a3")
    IA = steps("index_a", "rl0 rl1")
    IT = steps("index_t", "rope sc")
    JD = Steps([sem("sel_d")], "ki1 ki2 ki3 wi ka0 kb0 kc0 ka1 kb1 kc1 z cp " +
               " ".join(f"m{r}{b} r{r}{b}" for r in range(8) for b in range(2)) + " eq bi")
    JT = Steps([sem("sel_t")], "kd wt k0 k1")
    JA = Steps([sem("sel_a")], "s0 s1 s2 s3")
    JP = Steps([sem("sel_p")], "c0 c1 d0 d1")
    HD = Steps([sem("att_d")], "vf t0 u0 q0 vc t1 u1 q1 sm0 ma0 mb0 ng0 t2 u2 q2 sm1 ma1 mb1 ng1 rc0 na0 nb0 "
                               "t3 u3 q3 sm2 ma2 mb2 ng2 rc1 na1 nb1 lo0 sm3 ma3 mb3 ng3 rc2 na2 nb2 lo1 "
                               "rc3 na3 nb3 lo2 lo3")
    HA = Steps([sem("att_a")], "ea0 eb0 ea1 eb1 pc0 h0 ea2 eb2 pc1 h1 ea3 eb3 pc2 h2 pc3 h3")
    HT = Steps([sem("att_t")], "vt r0 r1 s0 r2 s1 pt0 o0 r3 s2 pt1 o1 s3 pt2 o2 pt3 o3")

    RWKV_ALL = len(RD.names) * 4

    def sync(sp):
        with sp.Fori(0, 4) as i:
            for g in lanes:
                RD.wait(sp, g, i, "r0")
                sp.dma_start(lw[g][:, :, :], A["lora"][bass.ds(2 * i + g, 1), :, :, :]
                             .rearrange("a p b c -> (a p) b c")).then_inc(lw_in[g], 16)
        for g in lanes:
            sp.wait_ge(RD.sems[g], RWKV_ALL)
        sp.dma_start(cm[:, :, :], A["const"][:, C_ROPE:C_ROPE + 4, :]).then_inc(cm_in, 16)

    def loads(act):
        act.dma_start(blk[:, :, :], A["const"][:, C_BLK1:C_BLK1 + 2, :]).then_inc(mk_in, 16)
        act.dma_start(mk[:, :, :], A["masks"]).then_inc(mk_in, 16)

    def gpsimd(pool):
        k = [0]

        def link(ins):
            ins.then_inc(tab_p, 1)
            k[0] += 1
            pool.wait_ge(tab_p, k[0])

        two_pi = 2 * np.pi
        c1 = 6.28125
        c2 = float(np.float32(two_pi - c1))
        c3 = float(two_pi - c1 - np.float64(np.float32(two_pi - c1)))
        magic = 12582912.0
        pool.wait_ge(e["evac_done"], e["p_done"])
        pool.dma_start(posi[:, :], A["pos"].to_broadcast([P, T])).then_inc(pos_in, 16)
        pool.wait_ge(pos_in, 16)
        pool.wait_ge(e["par_in"], 16)
        link(pool.tensor_copy(tp[:, 2, :], posi[:, :]))
        ang, rnd = tp[:, 0, :], tp[:, 1, :]
        for q in range(4):
            link(pool.tensor_scalar(ang, tp[:, 2, :], col("inv_freq", q // 2), None, ALU.mult))
            cosine = q % 2 == 0
            link(pool.tensor_scalar(rnd, ang, 1 / two_pi, 0.25 if cosine else 0.0, ALU.mult, ALU.add))
            link(pool.tensor_scalar(rnd, rnd, magic, None, ALU.add))
            link(pool.tensor_scalar(rnd, rnd, -magic, None, ALU.add))
            for c in (c1, c2, c3):
                link(pool.tensor_scalar(tab[:, q, :], rnd, -c, None, ALU.mult))
                link(pool.tensor_tensor(ang, ang, tab[:, q, :], ALU.add))
            link(pool.tensor_scalar(ang, ang, np.pi / 2 if cosine else 0.0, 3.1415925, ALU.add, ALU.min))
            link(pool.tensor_scalar(tab[:, q, :], ang, -3.1415925, None, ALU.max))
        for g in lanes:
            ID.wait(pool, g, 3, "a3")
        for b, (src, pre) in enumerate(((sc, "c"), (bias, "d"))):
            if b:
                JD.wait(pool, 0, 0, "bi")
            for tb in range(2):
                v = src[:, 0:P] if tb == 0 else src[:, P:384]
                JP.done(pool.affine_select(out=v, in_=v, pattern=[[-1, P * (tb + 1)]], compare_op=ALU.is_ge,
                                           fill=-1e30, base=P * tb, channel_multiplier=1), 0, f"{pre}{tb}")

    def scalar(act):
        act.wait_ge(pre_d, 6)
        act.activation(lx[0:64, 0, :], lx[0:64, 0, :], ACT.Tanh).then_inc(pre_a, 1)
        act.activation(lx[:, 1:3, :], lx[:, 1:3, :], ACT.Sigmoid).then_inc(pre_a, 1)
        with act.Fori(0, 4) as i:
            for g in lanes:
                n = 2 * i + g
                RT.wait(act, g, i, "lora")
                RA.done(act.activation(lda[g][:, 0, :], ps[:, 4 * g, 0:T], ACT.Sigmoid, bias=col("w0", n)), g, "sg")
                RA.done(act.activation(lda[g][:, 1, :], ps[:, 4 * g, T:2 * T], ACT.Sigmoid, bias=col("a0", n)), g, "aa")
                RA.done(act.activation(gg[g][:, :], ps[:, 4 * g + 1, 0:T], ACT.Copy), g, "gg")
            for g in lanes:
                RD.wait(act, g, i, "cp")
                RA.done(act.activation(dec[g][:, 0, :], cs[g][:, :], ACT.Exp), g, "e1")
                RA.done(act.activation(dec[g][:, 1, :], cs[g][:, :], ACT.Exp, scale=-1.0), g, "e2")
                RA.done(act.activation(dec[g][:, 2, :], lda[g][:, 0, :], ACT.Exp), g, "e3")
            for g in lanes:
                RD.wait(act, g, i, "km")
                RA.done(act.activation(rn[g][:, :], rn[g][:, :], ACT.Sqrt), g, "root")
            for g in lanes:
                RT.wait(act, g, i, "tr")
                RA.done(act.activation(tm[g][:, 0:2, :, :], ps[:, 4 * g + 2, :].rearrange("p (a b c) -> p a b c", a=2, b=2),
                                       ACT.Copy), g, "ta")
            for lv in range(1, 6):
                for g in lanes:
                    RT.wait(act, g, i, f"p{lv}")
                    RA.done(act.activation(pp[g][:, :, :], ps[:, 4 * g, :].rearrange("p (a b) -> p a b", a=4), ACT.Copy),
                            g, f"c{lv}")
            for g in lanes:
                RT.wait(act, g, i, "p5")
                for hd in range(2):
                    ins = act.activation(bt[g][:, 2 * hd:2 * hd + 2, 0:CH], tm[g][:, 0, :, CH * hd:CH * hd + CH], ACT.Copy)
                RA.done(ins, g, "za")
            for g in lanes:
                RT.wait(act, g, i, "au")
                RA.done(act.activation(pp[g][:, :, :], ps[:, 4 * g, :].rearrange("p (a b) -> p a b", a=4), ACT.Copy), g, "ac")
            for g in lanes:
                RT.wait(act, g, i, "ry")
                RA.done(act.activation(y1[g][:, :], ps[:, 4 * g + 2, 0:T], ACT.Copy), g, "y1")
            for g in lanes:
                RD.wait(act, g, i, "ve")
                RA.done(act.activation(rn[g][:, :], rn[g][:, :], ACT.Sqrt), g, "vr")
            for g in lanes:
                RD.wait(act, g, i, "yg")
                apart(act)
                RA.done(act.activation(one(act_in[:, bass.ds(2 * i + g, 1), 0:T]), rn[g][:, :], ACT.Copy), g, "hi")
        act.wait_ge(tab_p, 1 + 4 * 12)
        for q in range(4):
            JA.done(act.activation(tab[:, q, :], tab[:, q, :], ACT.Sin), 0, f"s{q}")
        with act.Fori(0, 4) as i:
            for g in lanes:
                IT.wait(act, g, i, "sc")
                for hd in range(2):
                    IA.done(act.activation(rel[g][:, hd, :], ps[:, 4 * g + 1 + hd, 0:384], ACT.Relu), g, f"rl{hd}")
        with act.Fori(0, 2) as i:
            for k in range(6):
                if k < 4:
                    HD.wait(act, 0, i, f"ng{k}")
                    for b in range(2):
                        v = sm[k % 2][:, 0:P] if b == 0 else sm[k % 2][:, P:384]
                        HA.done(act.activation(v, v, ACT.Exp, bias=sx_[:, k, b:b + 1], accum_out=sx_[:, k, 2 + b:3 + b]),
                                0, f"e{'ab'[b]}{k}")
                if 1 <= k <= 4:
                    q = k - 1
                    HT.wait(act, 0, i, f"pt{q}")
                    HA.done(act.activation(pt[q % 2][:, :, :], ps[:, 4 * (q % 2) + 2, 0:384]
                                           .rearrange("p (a b) -> p a b", a=3), ACT.Copy), 0, f"pc{q}")
                    HT.wait(act, 0, i, f"o{q}")
                    apart(act)
                    HA.done(act.activation(one(act_in[:, bass.ds(8 + 4 * i + q, 1), 0:T]), ps[:, 4 * (q % 2) + 3, 0:T],
                                           ACT.Copy), 0, f"h{q}")

    def shifted(dve, dst, tile, mu, first, second):
        if isinstance(tile, int):
            now, before = proj[:, tile, 1:TW], proj[:, tile, 0:T]
        else:
            now, before = one(proj[:, bass.ds(tile, 1), 1:TW]), one(proj[:, bass.ds(tile, 1), 0:T])
        first(dve.tensor_tensor(dst, before, now, ALU.subtract))
        second(dve.scalar_tensor_tensor(dst, dst, mu, now, ALU.mult, ALU.add))

    def vector(dve):
        c_half = float(np.exp(-0.5))
        dve.wait_ge(mk_in, 32)
        dve.wait_ge(e["evac_done"], e["p_done"])
        k = [0]

        def link(ins):
            ins.then_inc(pre_d, 1)
            k[0] += 1
            dve.wait_ge(pre_d, k[0])

        for q in range(3):
            shifted(dve, lx[:, q, :], T_LORA + q, col("mu", 24 + q), link, link)
        link(dve.tensor_scalar(omka, col("k_a", 0, RWT), -1.0, 1.0, ALU.mult, ALU.add))
        with dve.Fori(0, 4) as i:
            def do(g, name, ins, chain=True):
                RD.done(ins, g, name)
                if chain:
                    RD.wait(dve, g, i, name)
            for g in lanes:
                for q, x in enumerate("rkv"):
                    shifted(dve, rkv[g][:, q, :], 8 * q + 2 * i + g, col("mu", 8 * q + 2 * i + g),
                            lambda ins: do(g, x + "0", ins), lambda ins: do(g, x, ins))
            for g in lanes:
                do(g, "kr", dve.tensor_scalar(kk[g][:, :], rkv[g][:, 1, :], col("k_k", 2 * i + g), None, ALU.mult))
                do(g, "kq", dve.tensor_tensor(rn[g][:, :], kk[g][:, :], kk[g][:, :], ALU.mult), False)
            for g in lanes:
                RA.wait(dve, g, i, "aa")
                do(g, "ld", dve.tensor_scalar(lda[g][:, 0, :], lda[g][:, 0, :], -c_half, None, ALU.mult))
                do(g, "cs", dve.tensor_tensor_scan(cs[g][:, :], mk[:, 10:12, :].rearrange("p a b -> p (a b)"),
                                                   lda[g][:, 0, :], 0.0, ALU.mult, ALU.add))
                do(g, "cp", dve.tensor_tensor(lda[g][:, 0, :], cs[g][:, :], lda[g][:, 0, :], ALU.subtract), False)
            for g in lanes:
                RT.wait(dve, g, i, "kn")
                do(g, "km", dve.tensor_scalar(rn[g][:, :], ps[:, 4 * g + 1, T:2 * T], 1e-24, None, ALU.max), False)
            for g in lanes:
                n = 2 * i + g
                t = lambda q: tmp[g][:, q, :]
                RA.wait(dve, g, i, "root")
                do(g, "kv", dve.reciprocal(rn[g][:, :], rn[g][:, :]))
                do(g, "kk", dve.tensor_tensor(kk[g][:, :], kk[g][:, :], rn[g][:, :], ALU.mult))
                do(g, "am", dve.tensor_scalar(t(0), lda[g][:, 1, :], col("k_a", n), par[:, bass.ds(COL["spare"] + 16 + n, 1)],
                                              ALU.mult, ALU.add))
                do(g, "k2", dve.tensor_tensor(t(1), rkv[g][:, 1, :], t(0), ALU.mult))
                do(g, "bp", dve.scalar_tensor_tensor(t(2), rkv[g][:, 0, :], col("r_k", n), t(1), ALU.mult, ALU.mult))
            for g in lanes:
                t = lambda q: tmp[g][:, q, :]
                RT.wait(dve, g, i, "bs")
                do(g, "bo", dve.tensor_tensor(bo[g][:, :], ps[:, 4 * g + 2, 0:T], rkv[g][:, 2, :], ALU.mult), False)
                RA.wait(dve, g, i, "e3")
                do(g, "at", dve.scalar_tensor_tensor(ar[g][:, 0, :], kk[g][:, :], -1.0, dec[g][:, 2, :], ALU.mult, ALU.mult),
                   False)
                do(g, "rt", dve.tensor_tensor(ar[g][:, 1, :], rkv[g][:, 0, :], dec[g][:, 0, :], ALU.mult), False)
                do(g, "b0", dve.tensor_tensor(t(0), kk[g][:, :], lda[g][:, 1, :], ALU.mult))
                do(g, "bt", dve.tensor_tensor(bk[g][:, 0, :], t(0), dec[g][:, 1, :], ALU.mult), False)
                do(g, "kt", dve.tensor_tensor(bk[g][:, 1, :], t(1), dec[g][:, 1, :], ALU.mult), False)
            for g in lanes:
                RT.wait(dve, g, i, "tr")
                do(g, "tb", dve.tensor_copy(tm[g][:, 2:4, :, :], ps[:, 4 * g + 3, :]
                                            .rearrange("p (a b c) -> p a b c", a=2, b=2)), False)
            for g in lanes:
                RT.wait(dve, g, i, "ll")
                for u in range(4):
                    do(g, f"l{u}", dve.tensor_tensor(lm[g][:, u, :, :], ps[:, 4 * g + u, :].rearrange("p (a b) -> p a b", a=4),
                                                     mk[:, 0:4, :], ALU.mult), u == 3)

            def level(g, lv):
                return dve.tensor_tensor(bt[g][:, :, :], lm[g][:, :, 0, :],
                                         mk[:, 4 + lv:5 + lv, :].to_broadcast([P, 4, P]), ALU.mult)
            eye = ident[:, :].unsqueeze(1).to_broadcast([P, 4, P])
            bank = lambda g, b: ps[:, 4 * g + b, :].rearrange("p (a b) -> p a b", a=4)
            for g in lanes:
                do(g, "m0", level(g, 0))
            for g in lanes:
                RT.wait(dve, g, i, "p0")
                do(g, "x0", dve.tensor_tensor(xx[g][:, :, :], bank(g, 0), eye, ALU.add), False)
                do(g, "xt0", dve.tensor_tensor(xt[g][:, :, :], bt[g][:, :, :], eye, ALU.add))
                do(g, "m1", level(g, 1), False)
            for lv in range(1, 6):
                for g in lanes:
                    if lv < 5:
                        RT.wait(dve, g, i, f"p{lv}")
                        do(g, f"m{lv + 1}", level(g, lv + 1), False)
                    RT.wait(dve, g, i, f"q{lv}")
                    do(g, f"xt{lv}", dve.tensor_tensor(xt[g][:, :, :], bank(g, 1), xt[g][:, :, :], ALU.add), False)
                    if lv < 5:
                        do(g, f"x{lv}", dve.tensor_tensor(xx[g][:, :, :], bank(g, 2), xx[g][:, :, :], ALU.add))
            for g in lanes:
                RT.wait(dve, g, i, "w")
                do(g, "zw", dve.tensor_copy(bt[g][:, :, CH:P], ps[:, 4 * g + 3, 0:4 * CH].rearrange("p (a b) -> p a b", a=4)),
                   False)
            for g in lanes:
                RT.wait(dve, g, i, "ry")
                do(g, "r2", dve.tensor_tensor(r2[g][:, :], ps[:, 4 * g + 1, 0:T], ar[g][:, 1, :], ALU.add), False)
            for g in lanes:
                RT.wait(dve, g, i, "mn")
                b3, b0 = ps[:, 4 * g + 3, :], ps[:, 4 * g, :]
                do(g, "mt1", dve.tensor_tensor(mt[g][:, 0, :], b0[:, 0:CH], i64, ALU.add), False)
                do(g, "mt2", dve.tensor_tensor(mt[g][:, 1, :], b3[:, 0:CH], i64, ALU.add), False)
                for c, v in enumerate((b3[:, CH:2 * CH], b0[:, CH:2 * CH], b3[:, 2 * CH:3 * CH])):
                    last = CH * c + CH - 1
                    do(g, f"n{c}", dve.tensor_scalar(nn[g][:, c, :], v, dec[g][:, 0, last:last + 1], None, ALU.mult), c == 2)
            for c in (1, 2):
                for g in lanes:
                    RT.wait(dve, g, i, f"s{c}")
                    last = CH * c + CH - 1
                    for hd in range(2):
                        q = slice(CH * hd, CH * hd + CH)
                        do(g, f"s{c + 1}{'ab'[hd]}", dve.scalar_tensor_tensor(
                            st[g][q, c - 1, :], ps[q, 4 * g + 1 + hd, CH * (c - 1):CH * c], dec[g][q, 0, last:last + 1],
                            nn[g][q, c, :], ALU.mult, ALU.add), False)
            for g in lanes:
                RT.wait(dve, g, i, "yy")
                RA.wait(dve, g, i, "y1")
                for hd in range(2):
                    q = slice(CH * hd, CH * hd + CH)
                    do(g, f"y{'ab'[hd]}", dve.tensor_tensor(y1[g][q, CH:T], ps[q, 4 * g + 3 * hd, CH:T], y1[g][q, CH:T], ALU.add),
                       hd == 1)
            for g in lanes:
                RT.wait(dve, g, i, "mu")
                do(g, "yc", dve.tensor_tensor(y1[g][:, :], y1[g][:, :], ps[:, 4 * g + 1, T:2 * T], ALU.subtract))
                do(g, "yq", dve.tensor_tensor(rn[g][:, :], y1[g][:, :], y1[g][:, :], ALU.mult), False)
            for g in lanes:
                RT.wait(dve, g, i, "va")
                do(g, "ve", dve.tensor_scalar(rn[g][:, :], ps[:, 4 * g + 2, T:2 * T], EPS_HEAD, None, ALU.add), False)
            for g in lanes:
                n = 2 * i + g
                y = y1[g][:, :]
                RA.wait(dve, g, i, "vr")
                do(g, "vi", dve.reciprocal(rn[g][:, :], rn[g][:, :]))
                do(g, "yn", dve.tensor_tensor(y, y, rn[g][:, :], ALU.mult))
                do(g, "yw", dve.tensor_scalar(y, y, col("lnx_w", n), col("lnx_b", n), ALU.mult, ALU.add))
                do(g, "yo", dve.tensor_tensor(y, y, bo[g][:, :], ALU.add))
                do(g, "yg", dve.tensor_tensor(rn[g][:, :], y, gg[g][:, :], ALU.mult), False)
            for g in lanes:
                RA.wait(dve, g, i, "hi")
                ch = bass.ds(2 * i + g, 1)
                do(g, "lo", dve.tensor_tensor(one(act_in[:, ch, T:2 * T]), rn[g][:, :], one(act_in[:, ch, 0:T]).bitcast(F32),
                                              ALU.subtract), False)

        def jd(name, ins, chain=False):
            JD.done(ins, 0, name)
            if chain:
                JD.wait(dve, 0, 0, name)
        JA.wait(dve, 0, 0, "s3")
        JT.wait(dve, 0, 0, "kd")
        jd("ki1", dve.tensor_tensor(rt[0][:, 0, :], ps[:, 0, 0:T], tab[:, 2, :], ALU.mult))
        jd("ki2", dve.tensor_tensor(rt[0][:, 1, :], ps[:, 0, T:2 * T], tab[:, 3, :], ALU.mult), True)
        jd("ki3", dve.tensor_tensor(ki2[:, :], rt[0][:, 0, :], rt[0][:, 1, :], ALU.add))
        JT.wait(dve, 0, 0, "wt")
        jd("wi", dve.tensor_scalar(wi[:, :, :], ps[:, 1, 0:T].rearrange("p (a b) -> p a b", a=2)[:, :, 64:80], IDX_SCALE,
                                   None, ALU.mult))
        for v in range(2):
            JT.wait(dve, 0, 0, f"k{v}")
            key = proj[:, T_KA + v, 1:TW]
            jd(f"ka{v}", dve.tensor_tensor(rt[1][:, 0, :], ps[:, 2 + v, 0:T], tab[:, 1, :], ALU.mult))
            jd(f"kb{v}", dve.tensor_tensor(rt[1][:, 1, :], key, tab[:, 0, :], ALU.mult), True)
            jd(f"kc{v}", dve.tensor_tensor(key, rt[1][:, 0, :], rt[1][:, 1, :], ALU.add), True)
        jd("z", dve.memset(sc[:, :], 0.0), True)
        with dve.Fori(0, 4) as i:
            for g in lanes:
                IT.wait(dve, g, i, "rope")
                q = one(proj[:, bass.ds(T_QI + 2 * i + g, 1), 1:TW])
                ID.done(dve.tensor_tensor(rt[g][:, 0, :], ps[:, 4 * g, 0:T], tab[:, 3, :], ALU.mult), g, "t")
                ID.done(dve.tensor_tensor(rt[g][:, 1, :], q, tab[:, 2, :], ALU.mult), g, "u")
                ID.wait(dve, g, i, "u")
                ID.done(dve.tensor_tensor(qs[g][:, :], rt[g][:, 0, :], rt[g][:, 1, :], ALU.add), g, "q")
            for g in lanes:
                for hd in range(2):
                    IA.wait(dve, g, i, f"rl{hd}")
                    for b in range(2):
                        s = slice(0, P) if b == 0 else slice(P, 384)
                        ID.done(dve.scalar_tensor_tensor(sc[:, s], rel[g][:, hd, s],
                                                         one(wi[:, b:b + 1, bass.ds(4 * i + 2 * g + hd, 1)]), sc[:, s],
                                                         ALU.mult, ALU.add), g, f"a{2 * hd + b}")
                    ID.wait(dve, g, i, f"a{2 * hd + 1}")
        JP.wait(dve, 0, 0, "c1")
        jd("cp", dve.tensor_copy(wk[:, :], sc[:, :]), True)
        for r in range(8):
            for b in range(2):
                v = wk[:, 0:P] if b == 0 else wk[:, P:384]
                if r:
                    JD.wait(dve, 0, 0, f"r{r - 1}{b}")
                jd(f"m{r}{b}", dve.max(m8[:, b, :], v), True)
                jd(f"r{r}{b}", dve.match_replace(v, m8[:, b, :], v, -3e38))
        JD.wait(dve, 0, 0, "r71")
        jd("eq", dve.tensor_scalar(bias[:, :], wk[:, :], -3e38, None, ALU.is_equal), True)
        jd("bi", dve.tensor_scalar(bias[:, :], bias[:, :], 1e30, -1e30, ALU.mult, ALU.add))
        JP.wait(dve, 0, 0, "d1")
        with dve.Fori(0, 2) as i:
            def hd_(name, ins, chain=False):
                HD.done(ins, 0, name)
                if chain:
                    HD.wait(dve, 0, i, name)

            def rope(k):
                HT.wait(dve, 0, i, f"r{k}")
                q = one(proj[:, bass.ds(T_Q + 4 * i + k, 1), 1:TW])
                hd_(f"t{k}", dve.tensor_tensor(rt[k % 2][:, 0, :], ps[:, 4 * (k % 2), 0:T], tab[:, 1, :], ALU.mult))
                hd_(f"u{k}", dve.tensor_tensor(rt[k % 2][:, 1, :], q, tab[:, 0, :], ALU.mult), True)
                hd_(f"q{k}", dve.tensor_tensor(qs[k % 2][:, :], rt[k % 2][:, 0, :], rt[k % 2][:, 1, :], ALU.add))

            hd_("vf", dve.tensor_copy(vf[:, :], one(proj[:, bass.ds(T_VA + i, 1), 1:TW])))
            rope(0)
            HT.wait(dve, 0, i, "vt")
            hd_("vc", dve.tensor_copy(vs[:, :, :], ps[:, 3, 0:T].rearrange("p (a b) -> p a b", a=2)))
            for k in range(6):
                if k < 3:
                    rope(k + 1)
                if k < 4:
                    s = sm[k % 2]
                    HT.wait(dve, 0, i, f"s{k}")
                    if k >= 2:
                        HT.wait(dve, 0, i, f"pt{k - 2}")
                    hd_(f"sm{k}", dve.scalar_tensor_tensor(s[:, :], ps[:, 4 * (k % 2) + 1, 0:384], ATT_SCALE, bias[:, :],
                                                           ALU.mult, ALU.add), True)
                    hd_(f"ma{k}", dve.tensor_reduce(sx_[:, k, 0:1], s[:, 0:P], AX_X, ALU.max))
                    hd_(f"mb{k}", dve.tensor_reduce(sx_[:, k, 1:2], s[:, P:384], AX_X, ALU.max), True)
                    hd_(f"ng{k}", dve.tensor_scalar(sx_[:, k, 0:2], sx_[:, k, 0:2], -1.0, None, ALU.mult))
                if 1 <= k <= 4:
                    q = k - 1
                    HA.wait(dve, 0, i, f"eb{q}")
                    hd_(f"rc{q}", dve.reciprocal(sx_[:, q, 2:4], sx_[:, q, 2:4]), True)
                    hd_(f"na{q}", dve.tensor_scalar(sm[q % 2][:, 0:P], sm[q % 2][:, 0:P], sx_[:, q, 2:3], None, ALU.mult))
                    hd_(f"nb{q}", dve.tensor_scalar(sm[q % 2][:, P:384], sm[q % 2][:, P:384], sx_[:, q, 3:4], None, ALU.mult))
                if k >= 2:
                    q = k - 2
                    HA.wait(dve, 0, i, f"h{q}")
                    ch = bass.ds(8 + 4 * i + q, 1)
                    hd_(f"lo{q}", dve.tensor_tensor(one(act_in[:, ch, T:2 * T]), ps[:, 4 * (q % 2) + 3, 0:T],
                                                    one(act_in[:, ch, 0:T]).bitcast(F32), ALU.subtract))

    def tensor(pe):
        pe.wait_ge(pre_a, 2)
        pe.wait_ge(mk_in, 32)
        with pe.Fori(0, 4) as i:
            mm = pe.matmul
            for g in lanes:
                b = 4 * g
                RD.wait(pe, g, i, "r0")
                pe.wait_ge(lw_in[g], 16 * (i + 1))
                mm(ps[:, b, 0:T], lw[g][:, 0, :], lx[:, 0, :], start=True, stop=True)
                mm(ps[:, b, T:2 * T], lw[g][:, 1, :], lx[:, 0, :], start=True, stop=True)
                mm(ps[:, b + 1, 0:T], lw[g][:, 2, :], lx[:, 1, :], start=True, stop=False)
                RT.done(mm(ps[:, b + 1, 0:T], lw[g][:, 3, :], lx[:, 2, :], start=False, stop=True), g, "lora")
            for g in lanes:
                RD.wait(pe, g, i, "kq")
                RA.wait(pe, g, i, "gg")
                RT.done(mm(ps[:, 4 * g + 1, T:2 * T], blk[:, 0, :], rn[g][:, :], start=True, stop=True), g, "kn")
            for g in lanes:
                RD.wait(pe, g, i, "bp")
                RT.done(mm(ps[:, 4 * g + 2, 0:T], blk[:, 0, :], tmp[g][:, 2, :], start=True, stop=True), g, "bs")
            for g in lanes:
                RD.wait(pe, g, i, "kt")
                for q, src in enumerate((ar[g][:, 0, :], bk[g][:, 0, :], bk[g][:, 1, :], rkv[g][:, 2, :])):
                    for c in range(2):
                        at_ = (2 * (q % 2) + c) * P
                        ins = pe.transpose(ps[:, 4 * g + 2 + q // 2, at_:at_ + P], src[:, c * P:(c + 1) * P], ident[:, :])
                RT.done(ins, g, "tr")
            for g in lanes:
                RA.wait(pe, g, i, "ta")
                RD.wait(pe, g, i, "tb")
                for u in range(4):
                    q, c = slice(CH * (u // 2), CH * (u // 2) + CH), slice((u % 2) * P, (u % 2) * P + P)
                    for w in range(2):
                        ins = mm(ps[:, 4 * g + u, w * T:(w + 1) * T], bk[g][q, w, c], ar[g][q, :, c], start=True, stop=True)
                RT.done(ins, g, "ll")
            for g in lanes:
                RD.wait(pe, g, i, "m0")
                for u in range(4):
                    ins = pe.transpose(ps[:, 4 * g, u * P:(u + 1) * P], bt[g][:, u, :], ident[:, :])
                RT.done(ins, g, "p0")
            for lv in range(1, 6):
                for g in lanes:
                    RD.wait(pe, g, i, "m1" if lv == 1 else f"x{lv - 1}")
                    for u in range(4):
                        ins = mm(ps[:, 4 * g, u * P:(u + 1) * P], bt[g][:, u, :], xx[g][:, u, :], start=True, stop=True)
                    RT.done(ins, g, f"p{lv}")
                for g in lanes:
                    RA.wait(pe, g, i, f"c{lv}")
                    for u in range(4):
                        at_ = slice(u * P, (u + 1) * P)
                        ins = mm(ps[:, 4 * g + 1, at_], pp[g][:, u, :], xt[g][:, u, :], start=True, stop=True)
                        if lv < 5:
                            ins = mm(ps[:, 4 * g + 2, at_], xt[g][:, u, :], pp[g][:, u, :], start=True, stop=True)
                    RT.done(ins, g, f"q{lv}")
            for g in lanes:
                for u in range(4):
                    ins = mm(ps[:, 4 * g + 3, u * CH:(u + 1) * CH], lm[g][:, u, 2, :],
                             tm[g][:, 3, u % 2, CH * (u // 2):CH * (u // 2) + CH], start=True, stop=True)
                RT.done(ins, g, "w")
            for g in lanes:
                RA.wait(pe, g, i, "za")
                RD.wait(pe, g, i, "zw")
                for u in range(4):
                    ins = mm(ps[:, 4 * g, u * P:(u + 1) * P], xt[g][:, u, :], bt[g][:, u, :], start=True, stop=True)
                RT.done(ins, g, "au")
            for g in lanes:
                RA.wait(pe, g, i, "ac")
                for u in range(4):
                    q, c = slice(CH * (u // 2), CH * (u // 2) + CH), slice((u % 2) * P, (u % 2) * P + P)
                    mm(ps[q, 4 * g + 1, c], pp[g][:, u, 0:CH], lm[g][:, u, 1, :], start=True, stop=True)
                    mm(ps[q, 4 * g + 2, c], pp[g][:, u, CH:P], lm[g][:, u, 1, :], start=True, stop=False)
                    ins = mm(ps[q, 4 * g + 2, c], tm[g][:, 3, u % 2, q], lm[g][:, u, 3, :], start=False, stop=True)
                RT.done(ins, g, "ry")
            for g in lanes:
                for c in range(3):
                    o = slice(CH * (c % 2), CH * (c % 2) + CH)
                    bank = 4 * g + (0 if c == 1 else 3)
                    n_at = (1, 1, 2)[c] * CH
                    for hd in range(2):
                        q, u = slice(CH * hd, CH * hd + CH), 2 * hd + c // 2
                        if c:
                            mm(ps[q, bank, 0:CH], pp[g][o, u, 0:CH], tm[g][o, 1, c // 2, q], start=True, stop=True)
                        mm(ps[q, bank, n_at:n_at + CH], tm[g][o, 1, c // 2, q], pp[g][o, u, CH:P], start=True, stop=False)
                        ins = mm(ps[q, bank, n_at:n_at + CH], tm[g][o, 2, c // 2, q], tm[g][o, 3, c // 2, q],
                                 start=False, stop=True)
                RT.done(ins, g, "mn")
            for c in (1, 2):
                for g in lanes:
                    RD.wait(pe, g, i, "n2" if c == 1 else "s2b")
                    if c == 1:
                        RA.wait(pe, g, i, "y1")
                    apart(pe)
                    for hd in range(2):
                        q = slice(CH * hd, CH * hd + CH)
                        s = nn[g][q, 0, :] if c == 1 else st[g][q, 0, :]
                        ins = mm(ps[q, 4 * g + 1 + hd, CH * (c - 1):CH * c], mt[g][q, c - 1, :], s, start=True, stop=True)
                    RT.done(ins, g, f"s{c}")
            for g in lanes:
                RD.wait(pe, g, i, "s3b")
                apart(pe)
                for hd in range(2):
                    q = slice(CH * hd, CH * hd + CH)
                    for c in range(1, 4):
                        s = nn[g][q, 0, :] if c == 1 else st[g][q, c - 2, :]
                        ins = mm(ps[q, 4 * g + 3 * hd, CH * c:CH * c + CH], s, r2[g][q, CH * c:CH * c + CH],
                                 start=True, stop=True)
                RT.done(ins, g, "yy")
            for g in lanes:
                RD.wait(pe, g, i, "yb")
                RT.done(mm(ps[:, 4 * g + 1, T:2 * T], blk[:, 1, :], y1[g][:, :], start=True, stop=True), g, "mu")
            for g in lanes:
                RD.wait(pe, g, i, "yq")
                RT.done(mm(ps[:, 4 * g + 2, T:2 * T], blk[:, 1, :], rn[g][:, :], start=True, stop=True), g, "va")

        for g in lanes:
            pe.wait_ge(RD.sems[g], RWKV_ALL)
        pe.wait_ge(cm_in, 16)
        ki = proj[:, T_KI, 1:TW]
        pe.matmul(ps[:, 0, 0:T], cm[:, 2, :], ki, start=True, stop=True)
        JT.done(pe.matmul(ps[:, 0, T:2 * T], cm[:, 3, :], ki, start=True, stop=True), 0, "kd")
        for b in range(2):
            ins = pe.transpose(ps[:, 1, b * P:(b + 1) * P], proj[:, T_KI, 1 + b * P:1 + (b + 1) * P], ident[:, :])
        JT.done(ins, 0, "wt")
        for v in range(2):
            JT.done(pe.matmul(ps[:, 2 + v, 0:T], cm[:, 0, :], proj[:, T_KA + v, 1:TW], start=True, stop=True), 0, f"k{v}")
        JD.wait(pe, 0, 0, "z")
        with pe.Fori(0, 4) as i:
            for g in lanes:
                JD.wait(pe, 0, 0, "z")
                IT.done(pe.matmul(ps[:, 4 * g, 0:T], cm[:, 1, :], one(proj[:, bass.ds(T_QI + 2 * i + g, 1), 1:TW]),
                                  start=True, stop=True), g, "rope")
            for g in lanes:
                ID.wait(pe, g, i, "q")
                for hd in range(2):
                    q = slice(CH * hd, CH * hd + CH)
                    for b in range(2):
                        ins = pe.matmul(ps[:, 4 * g + 1 + hd, b * P:b * P + P * (b + 1)], qs[g][q, b * P:(b + 1) * P],
                                        ki2[q, 0:P * (b + 1)], start=True, stop=True)
                IT.done(ins, g, "sc")
        with pe.Fori(0, 2) as i:
            def rope(k):
                if k >= 2:
                    HD.wait(pe, 0, i, f"t{k - 2}")
                HT.done(pe.matmul(ps[:, 4 * (k % 2), 0:T], cm[:, 0, :], one(proj[:, bass.ds(T_Q + 4 * i + k, 1), 1:TW]),
                                  start=True, stop=True), 0, f"r{k}")
            HD.wait(pe, 0, i, "vf")
            for b in range(2):
                ins = pe.transpose(ps[:, 3, b * P:(b + 1) * P], vf[:, b * P:(b + 1) * P], ident[:, :])
            HT.done(ins, 0, "vt")
            rope(0)
            for k in range(5):
                if k < 3:
                    rope(k + 1)
                if k < 4:
                    HD.wait(pe, 0, i, f"q{k}")
                    for b in range(2):
                        ins = pe.matmul(ps[:, 4 * (k % 2) + 1, b * P:b * P + P * (b + 1)], qs[k % 2][:, b * P:(b + 1) * P],
                                        one(proj[:, bass.ds(T_KA + i, 1), 1:1 + P * (b + 1)]), start=True, stop=True)
                    HT.done(ins, 0, f"s{k}")
                if k >= 1:
                    q = k - 1
                    HD.wait(pe, 0, i, f"nb{q}")
                    for b in range(3):
                        ins = pe.transpose(ps[:, 4 * (q % 2) + 2, b * P:(b + 1) * P], sm[q % 2][:, b * P:(b + 1) * P],
                                           ident[:, :])
                    HT.done(ins, 0, f"pt{q}")
                    HA.wait(pe, 0, i, f"pc{q}")
                    o = ps[:, 4 * (q % 2) + 3, :]
                    pe.matmul(o[:, 0:P], vs[:, 0, :], pt[q % 2][:, 0, :], start=True, stop=True)
                    pe.matmul(o[:, P:T], vs[:, 0, :], pt[q % 2][:, 1, :], start=True, stop=False)
                    HT.done(pe.matmul(o[:, P:T], vs[:, 1, :], pt[q % 2][:, 2, :], start=False, stop=True), 0, f"o{q}")

    return dict(sync=sync, gpsimd=gpsimd, scalar=scalar, vector=vector, tensor=tensor, loads=loads,
                lo=HD.sems[0], lo_all=2 * len(HD.names))


def schedule(loop, iters, lens, split, evac):
    S = sum(lens)
    due, end = {}, 0
    for g, ln in enumerate(lens):
        end += ln
        for t in range(4):
            due.setdefault(end + 1 + (t * ln) // 8, []).append((g, t))
    R = max(due) - S + 1
    for p in range(R):
        split(0, p)

    def body(i, last):
        for p in range(R, S + R):
            if p < S:
                split(i, p)
            elif not last:
                split(i + 1, p - S)
            for g, t in due.get(p, ()):
                evac(i, g, t)

    loop(iters, body)


def looped(eng):
    def loop(iters, body):
        if iters > 1:
            with eng.Fori(0, iters - 1) as i:
                body(i, False)
        body(iters - 1, True)
    return loop


def staged(t, *stages):
    for s, f in enumerate(stages):
        if t >= s and f:
            f(t - s)
    if t == 3:
        for q in range(1, len(stages)):
            for s in range(q, len(stages)):
                if stages[s]:
                    stages[s](3 - (s - q))


class Lin:

    def __init__(self, n0, g0, lens, iters):
        self.n0, self.g0, self.lens, self.iters, self.S = n0, g0, lens, iters, sum(lens)
        self.ends = [sum(lens[:k + 1]) for k in range(len(lens))]
        assert n0 % RING == 0 and self.S % RING == 0 and (iters == 1 or len(lens) % 2 == 0)

    def slot(self, i, p):
        return self.n0 + i * self.S + p

    def group(self, i, g):
        return self.g0 + i * len(self.lens) + g

    def tile(self, i, g, t):
        return 4 * self.group(i, g) + t

    def bank(self, g, t):
        return 4 * ((self.g0 + g) % 2) + t


def build(nc, A, out):
    ctx = ExitStack()

    def sem(name):
        return ctx.enter_context(nc.semaphore(name))

    def sems(names):
        return [sem(x) for x in names.split()]

    base = (nc.sbuf_base + 31) // 32 * 32
    room = nc.sbuf_usable_end - base - 32
    nc.alloc_sbuf_tensor("arena", [P, room], U8)
    K = 1024

    def at(name, shape, off, dt=F32, end=None):
        size = 4
        for d in shape[1:]:
            size *= d
        assert off + size <= (room if end is None else end), (name, off, size)
        return nc.alloc_sbuf_tensor_at(name, shape, dt, offset=base + off)

    O_RAW, O_HI, O_LO, O_XN, O_ACT, O_P = 16 * K, 32 * K, 48 * K, 64 * K, 96 * K, 128 * K
    O_KV = O_P + (NT * TW * 4 + 31) // 32 * 32
    O_ADA = O_KV + 8 * K
    O_PAR = O_ADA + 8 * K
    O_TMP = O_PAR + (NPAR * 4 + 31) // 32 * 32
    h = at("h", [P, DC, T], 0)
    raw = at("raw", [P, RING, SLOT], O_RAW)
    whi = at("whi", [P, RING, SLOT], O_HI, F32R)
    wlo = at("wlo", [P, RING, SLOT], O_LO, F32R)
    xn = at("xn", [P, DC, 2 * T], O_XN, F32R)
    act_in = at("act_in", [P, DC, 2 * T], O_ACT, F32R)
    proj = at("proj", [P, NT, TW], O_P)
    kv = at("kv", [P, 8, T], O_KV)
    adaw = at("adaw", [P, 2, SLOT], O_ADA)
    par = at("par", [P, NPAR], O_PAR)
    hl = at("hl", [P, 4, T], O_TMP)
    tt = at("tt", [P, 4, T], O_TMP + 4 * K)
    ss = at("ss", [P, T], O_TMP + 8 * K)
    rstd = at("rstd", [P, T], O_TMP + 9 * K)
    ident = at("ident", [P, P], O_TMP + 10 * K)
    ones = at("ones", [P, P], O_TMP + 10 * K + 512)
    mod = at("mod", [P, 96 + 2 * DC], O_TMP + 11 * K)
    silu_c = at("silu_c", [P, DC], O_TMP + 11 * K + 512)
    zero = at("zero", [P, 1], O_TMP + 11 * K + 576)
    ada = at("ada", [P, 24, 512], O_P)
    memx = at("memx", [P, DC, T], O_P + 32 * K)
    qx = at("qx", [P, 4, T], O_P + 32 * K)
    vx = at("vx", [P, 4, 2, P], O_P + 36 * K)
    sx = at("sx", [P, 2, 2, T], O_P + 40 * K)
    pxt = at("pxt", [P, 2, 4, P], O_P + 44 * K)
    stx = at("stx", [P, 4, 4], O_PAR + 4 * (COL["spare"]))
    vmix = at("vmix", [P, AWC, T], O_P)
    vstat = at("vstat", [P, 2, 2, T], O_P + 32 * K)
    vtok = at("vtok", [P, 2, 4, P], O_P + 36 * K)
    wst = at("wst", [P, 16, P], O_P + 40 * K, end=O_KV)
    bsb = at("bsb", [P, 16, P], O_KV)
    zc = at("zc", [P, 4, T + 2], O_P)
    yc = at("yc", [P, 4, T], O_P + 8 * K)
    fin = at("fin", [P, DC, T], O_P + 16 * K)
    ps = ctx.enter_context(nc.psum_tensor("ps", [P, 8, 512], F32))

    def col(name, j=0, n=1):
        c = COL[name] + j
        return par[:, bass.ds(c, n)] if not isinstance(c, int) else par[:, c:c + n]

    def one(x):
        return x.rearrange("p a c -> p (a c)")

    L, n, g = {}, 0, 0
    for name, it, lens in [("w_in", 6, [8, 8]), ("mix_out", 1, [8] * 4), ("kv", 1, [8, 8]), ("q", 1, [8]),
                           ("o", 1, [2] * 4), ("mlp", 4, [8] * 8), ("a_v", 4, [8, 8]), ("a_uo", 2, [8] * 8),
                           ("ffn", 2, [8] * 12), ("ffn_tail", 1, [8] * 6 + [6] * 4)]:
        L[name] = Lin(n, g, lens, it)
        n += it * sum(lens)
        g += it * len(lens)
    NSLOT = n
    ADA_AT = {"mix_out": (0, 4), "kv": (32, 4), "q": (48, 4), "o": (56, 4), "mlp": (64, 2)}

    w_landed = [sem(f"w_landed{r}") for r in range(RING)]
    ada_landed = [sem(f"ada_landed{r}") for r in range(2)]
    hi_done, lo_done, slot_used, tile_done, hl_done, evac_done = sems(
        "hi_done lo_done slot_used tile_done hl_done evac_done")
    ada_sum, ada_red, mod_done = sems("ada_sum ada_red mod_done")
    par_in, h_in, const_in, mem_in, mix_in, out_in = sems("par_in h_in const_in mem_in mix_in out_in")
    sq_done, ss_done, stat_done, rt_done, rs_done, rstd_done = sems(
        "sq_done ss_done stat_done rt_done rs_done rstd_done")
    xp_done, xh_done, xn_ready = sems("xp_done xh_done xn_ready")
    h_sum, r_done, ah_done, ai_ready, g_done, v_done = sems("h_sum r_done ah_done ai_ready g_done v_done")
    cols_zero, silu_done, h_normed, fin_done = sems("cols_zero silu_done h_normed fin_done")
    x_t, x_a, x_d = sems("x_t x_a x_d")
    m_t, m_a, m_d = sems("m_t m_a m_d")
    y_done, y_sum, s_done, pads = sems("y_done y_sum s_done pads")

    NORM = {nm: k for k, nm in enumerate(["mix", "mem", "cross", "mlp", "final", "g0", "av", "g1", "out"])}
    SQ, k = {}, 0
    for nm, c in [("mix", 16), ("mem", 16), ("cross", 16), ("mlp", 16), ("final", 64), ("g0", 16), ("av", 32),
                  ("g1", 32), ("out", 48)]:
        SQ[nm] = (k, k + c)
        k += c
    XP = {nm: 16 * k for k, nm in enumerate(["mix", "mem", "cross", "mlp", "g0", "g1"])}
    HS = {"mix_out": (0, "cross"), "o": (16, "mlp"), "mlp": (32, "final"), "a_uo": (96, "g1"),
          "ffn": (128, "out"), "ffn_tail": (160, "out")}
    SQ_AT = {"mix_out": SQ["cross"][0], "o": SQ["mlp"][0], "mlp": SQ["final"][0], "a_uo": SQ["g1"][0],
             "ffn": SQ["out"][0], "ffn_tail": SQ["out"][0] + 32}
    AI = {"mlp": 0, "a_uo": 64, "ffn": 96, "ffn_tail": 128}

    def apart(eng):
        eng.nop(nofuse=True)

    mixer = make_mixers(nc, at, sem, A, K, dict(O_HI=O_HI, O_ACT=O_ACT, O_KV=O_KV, proj=proj, par=par,
                                                col=col, one=one, ps=ps, ident=ident, act_in=act_in,
                                                evac_done=evac_done, apart=apart, par_in=par_in,
                                                O_HL=O_TMP,
                                                p_done=8 + 4 * 12))

    stat_bank = {nm: L[ph].bank(0, 0) for nm, ph in [("mix", "w_in"), ("mem", "mix_out"), ("cross", "q"),
                                                     ("mlp", "mlp"), ("final", "a_v"), ("g0", "a_v"), ("av", "a_uo"),
                                                     ("g1", "ffn")]}
    stat_bank["out"] = L["ffn_tail"].bank(10, 0)
    ada_bank = stat_bank["final"] + 1
    FT = {"ffn": 0, "ffn_tail": 64}
    FC = {"ffn": 0, "ffn_tail": 32}

    def tile_wait(eng, lin, i, g, t):
        if t < 3:
            eng.wait_ge(tile_done, 3 * lin.group(i, g) + t + 1)
        else:
            eng.wait_ge(slot_used, lin.slot(i, lin.ends[g]) + RING)

    XT = Steps([x_t], "vt0 vt1 s0 s1 pt0 o0 s2 pt1 o1 s3 pt2 o2 pt3 o3")
    XA = Steps([x_a], "v0 e00 e01 e10 e11 pc0 h0 e20 e21 pc1 h1 e30 e31 pc2 h2 pc3 h3")
    XD = Steps([x_d], "v1 sm0 mx0 ng0 sm1 mx1 ng1 rc0 na0 nb0 sm2 mx2 ng2 rc1 na1 nb1 lo0 sm3 mx3 ng3 rc2 na2 nb2 lo1 "
                      "rc3 na3 nb3 lo2 lo3")

    def cross_scalar(act):
        XT.wait(act, 0, 0, "vt0")
        XA.done(act.activation(vx[:, 0:2, :, :], ps[:, 3, :].rearrange("p (a b c) -> p a b c", a=2, b=2), ACT.Copy),
                0, "v0")
        for k in range(6):
            if k < 4:
                XD.wait(act, 0, 0, f"ng{k}")
                for b in range(2):
                    XA.done(act.activation(sx[:, k % 2, b, :], sx[:, k % 2, b, :], ACT.Exp,
                                           bias=stx[:, k, b:b + 1], accum_out=stx[:, k, 2 + b:3 + b]), 0, f"e{k}{b}")
            if k in (1, 2, 3, 4):
                q = k - 1
                XT.wait(act, 0, 0, f"pt{q}")
                XA.done(act.activation(pxt[:, q % 2, :, :], ps[:, 4 * (q % 2) + 1, :].rearrange("p (a b) -> p a b", a=4),
                                       ACT.Copy), 0, f"pc{q}")
                XT.wait(act, 0, 0, f"o{q}")
                XA.done(act.activation(act_in[:, q, 0:T], ps[:, 4 * (q % 2) + 2, 0:T], ACT.Copy), 0, f"h{q}")

    def cross_vector(dve):
        XT.wait(dve, 0, 0, "vt1")
        XD.done(dve.tensor_copy(vx[:, 2:4, :, :], ps[:, 7, :].rearrange("p (a b c) -> p a b c", a=2, b=2)), 0, "v1")
        for k in range(6):
            if k < 4:
                XT.wait(dve, 0, 0, f"s{k}")
                if k >= 2:
                    XT.wait(dve, 0, 0, f"pt{k - 2}")
                XD.done(dve.tensor_scalar(sx[:, k % 2, :, :], ps[:, 4 * (k % 2), :].rearrange("p (a b) -> p a b", a=2),
                                          ATT_SCALE, None, ALU.mult), 0, f"sm{k}")
                XD.wait(dve, 0, 0, f"sm{k}")
                XD.done(dve.tensor_reduce(stx[:, k, 0:2], sx[:, k % 2, :, :], AX_X, ALU.max), 0, f"mx{k}")
                XD.wait(dve, 0, 0, f"mx{k}")
                XD.done(dve.tensor_scalar(stx[:, k, 0:2], stx[:, k, 0:2], -1.0, None, ALU.mult), 0, f"ng{k}")
            if 1 <= k <= 4:
                q = k - 1
                XA.wait(dve, 0, 0, f"e{q}1")
                XD.done(dve.reciprocal(stx[:, q, 2:4], stx[:, q, 2:4]), 0, f"rc{q}")
                XD.wait(dve, 0, 0, f"rc{q}")
                for b in range(2):
                    XD.done(dve.tensor_scalar(sx[:, q % 2, b, :], sx[:, q % 2, b, :], stx[:, q, 2 + b:3 + b], None,
                                              ALU.mult), 0, f"n{'ab'[b]}{q}")
            if k >= 2:
                q = k - 2
                XA.wait(dve, 0, 0, f"h{q}")
                XD.done(dve.tensor_tensor(act_in[:, q, T:2 * T], ps[:, 4 * (q % 2) + 2, 0:T],
                                          act_in[:, q, 0:T].bitcast(F32), ALU.subtract), 0, f"lo{q}")

    def cross_tensor(pe):
        for b in range(2):
            for hh in range(2):
                for m in range(2):
                    ins = pe.transpose(ps[:, 4 * b + 3, (2 * hh + m) * P:(2 * hh + m + 1) * P],
                                       kv[:, 4 + 2 * b + hh, m * P:(m + 1) * P], ident[:, :])
            XT.done(ins, 0, f"vt{b}")

        def scores(k):
            if k >= 2:
                XD.wait(pe, 0, 0, f"sm{k - 2}")
            for b in range(2):
                ins = pe.matmul(ps[:, 4 * (k % 2), b * T:(b + 1) * T], qx[:, k, b * P:(b + 1) * P], kv[:, k, :],
                                start=True, stop=True)
            XT.done(ins, 0, f"s{k}")

        scores(0)
        scores(1)
        for k in range(4):
            XD.wait(pe, 0, 0, f"nb{k}")
            for b in range(2):
                for m in range(2):
                    ins = pe.transpose(ps[:, 4 * (k % 2) + 1, (2 * m + b) * P:(2 * m + b + 1) * P],
                                       sx[:, k % 2, b, m * P:(m + 1) * P], ident[:, :])
            XT.done(ins, 0, f"pt{k}")
            XA.wait(pe, 0, 0, f"pc{k}")
            XA.wait(pe, 0, 0, "v0")
            XD.wait(pe, 0, 0, "v1")
            if k >= 2:
                XD.wait(pe, 0, 0, f"lo{k - 2}")
            for m in range(2):
                ins = pe.matmul(ps[:, 4 * (k % 2) + 2, 0:T], vx[:, k, m, :],
                                pxt[:, k % 2, 2 * m:2 * m + 2, :].rearrange("p a b -> p (a b)"),
                                start=m == 0, stop=m == 1)
            XT.done(ins, 0, f"o{k}")
            if k < 2:
                scores(k + 2)

    MT = Steps(sems("mix_t0 mix_t1"), "turn mix")
    MA = Steps(sems("mix_a0 mix_a1"), "turned")
    MD = Steps(sems("mix_d0 mix_d1"), "scaled s0 s1")

    def mixing_scalar(act):
        with act.Fori(0, 8) as i:
            for r in range(2):
                MT.wait(act, r, i, "turn")
                MA.done(act.activation(vtok[:, r, :, :], ps[:, 4 * r, :].rearrange("p (a b) -> p a b", a=4), ACT.Copy),
                        r, "turned")

    def mixing_vector(dve):
        with dve.Fori(0, 8) as i:
            for r in range(2):
                MD.done(dve.tensor_tensor(vstat[:, r, :, :], vmix[:, bass.ds(4 * i + 2 * r, 2), :],
                                          rstd[:, :].unsqueeze(1).to_broadcast([P, 2, T]), ALU.mult), r, "scaled")
            for r in range(2):
                MT.wait(dve, r, i, "mix")
                for q in range(2):
                    MD.done(dve.scalar_tensor_tensor(
                        vmix[:, bass.ds(4 * i + 2 * r + q, 1), :].rearrange("p a (n t) -> p (a n) t", n=2),
                        ps[:, 4 * r + 1, q * T:(q + 1) * T].rearrange("p (n t) -> p n t", n=2),
                        col("g_v", 4 * i + 2 * r + q),
                        bsb[:, bass.ds(2 * i + r, 1), :].to_broadcast([P, 2, P]), ALU.mult, ALU.add), r, f"s{q}")

    def mixing_tensor(pe):
        with pe.Fori(0, 8) as i:
            for r in range(2):
                MD.wait(pe, r, i, "scaled")
                for q in range(2):
                    for c in range(2):
                        ins = pe.transpose(ps[:, 4 * r, (2 * q + c) * P:(2 * q + c + 1) * P],
                                           vstat[:, r, q, c * P:(c + 1) * P], ident[:, :])
                MT.done(ins, r, "turn")
            for r in range(2):
                MA.wait(pe, r, i, "turned")
                for q in range(4):
                    ins = pe.matmul(ps[:, 4 * r + 1, q * P:(q + 1) * P], vtok[:, r, q, :],
                                    one(wst[:, bass.ds(2 * i + r, 1), :]), start=True, stop=True)
                MT.done(ins, r, "mix")

    block = ctx.enter_context(nc.Block())

    @block.sync
    def _(sp):
        for q in range(4):
            sp.dma_start(h[:, 4 * q:4 * q + 4, :], A["xT"][:, 4 * q:4 * q + 4, :]).then_inc(h_in, 16)

        def load(n, r):
            sp.wait_ge(lo_done, n + 1)
            sp.dma_start(raw[:, r, :], A["stream"][bass.ds(n, 1), :, :].rearrange("a p c -> (a p) c"))\
              .then_inc(w_landed[r], 16)

        def load_ada(m, r):
            sp.wait_ge(ada_sum, 2 * m + 1)
            sp.dma_start(adaw[:, r, :], A["ada"][bass.ds(m, 1), :, :].rearrange("a p c -> (a p) c"))\
              .then_inc(ada_landed[r], 16)

        def stream(n0, n1, ada0=0, per=0):
            with sp.Fori(0, (n1 - n0) // 4) as q:
                for r in range(4):
                    load(n0 + 4 * q + r, r)
                    if per == 4 or (per == 2 and r % 2):
                        a = r if per == 4 else r // 2
                        load_ada(ada0 + per * q + a, a % 2)

        first = L["mix_out"].n0
        stream(0, first)
        for r in range(RING):
            load(first + r, r)
        mixer["sync"](sp)
        sp.wait_ge(mixer["lo"], mixer["lo_all"])
        for m in range(4):
            load_ada(m, m % 2)
        for nm, nxt in [("mix_out", "kv"), ("kv", "q"), ("q", "o"), ("o", "mlp"), ("mlp", "a_v")]:
            if nm == "mix_out":
                stream(first + 4, L[nxt].n0, 4, 4)
            else:
                stream(L[nm].n0, L[nxt].n0, *ADA_AT[nm])
        stream(L["a_v"].n0, NSLOT)
        for q in range(4):
            sp.wait_ge(fin_done, 4 * q + 4)
            sp.dma_start(out[:, 4 * q:4 * q + 4, :], fin[:, 4 * q:4 * q + 4, :]).then_inc(out_in, 16)
        sp.wait_ge(out_in, 64)

    @block.gpsimd
    def _(pool):
        pool.memset(proj[:, :, 0:1], 0.0).then_inc(cols_zero, 1)
        pool.memset(zero[:, :], 0.0).then_inc(cols_zero, 1)

        def sum_squares(nm, reps, tiles=16):
            n0 = SQ[nm][0]
            if NORM[nm] > 0:
                pool.wait_ge(stat_done, NORM[nm])

            def body(i, _):
                for q in range(tiles):
                    m = n0 + tiles * i + q
                    pool.wait_ge(sq_done, m + 1)
                    if not isinstance(m, int) or m > 0:
                        pool.wait_ge(ss_done, m)
                    if q == 0:
                        apart(pool)
                        pool.tensor_copy(ss[:, :], tt[:, 0, :]).then_inc(ss_done, 1)
                    else:
                        pool.tensor_tensor(ss[:, :], ss[:, :], tt[:, q % 4, :], ALU.add).then_inc(ss_done, 1)

            looped(pool)(reps, body)

        sum_squares("mix", 1)
        mixer["gpsimd"](pool)
        sum_squares("mem", 1)
        sum_squares("cross", 1)
        sum_squares("mlp", 1)
        sum_squares("final", 4)
        sum_squares("g0", 1)
        sum_squares("av", 1, 32)
        sum_squares("g1", 2)
        sum_squares("out", 3)

    @block.scalar
    def _(act):
        act.dma_start(par[:, :], A["par"]).then_inc(par_in, 16)
        act.dma_start(ident[:, :], A["const"][:, C_ID, :]).then_inc(const_in, 16)
        act.dma_start(ones[:, :], A["const"][:, C_ONES, :]).then_inc(const_in, 16)
        mixer["loads"](act)
        loop = looped(act)

        def split(lin):
            def f(i, p):
                r = p % RING
                act.wait_ge(w_landed[r], 16 * (lin.n0 // 4 + i * (lin.S // 4) + p // 4 + 1))
                act.wait_ge(slot_used, lin.slot(i, p) + 1)
                act.activation(whi[:, r, :], raw[:, r, :], ACT.Copy).then_inc(hi_done, 1)
            return f

        def half(lin, i, g, t):
            tile_wait(act, lin, i, g, t)
            act.wait_ge(evac_done, lin.tile(i, g, t) + 5)
            act.activation(hl[:, t, :], ps[:, lin.bank(g, t), T:2 * T], ACT.Copy).then_inc(hl_done, 1)

        def squares(src, n0):
            for j in range(DC):
                if n0 + j >= 4:
                    act.wait_ge(ss_done, n0 + j - 3)
                act.activation(tt[:, j % 4, :], src[:, j, :], ACT.Square).then_inc(sq_done, 1)

        def norm(nm):
            act.wait_ge(rt_done, NORM[nm] + 1)
            act.activation(rstd[:, :], rstd[:, :], ACT.Sqrt).then_inc(rs_done, 1)

        def prepare(nm, shift=None):
            for j in range(DC):
                act.wait_ge(xp_done, XP[nm] + j + 1)
                b = zero[:, :] if shift is None else mod[:, shift + j:shift + j + 1]
                act.activation(xn[:, j, 0:T], tt[:, j % 4, :], ACT.Identity, bias=b).then_inc(xh_done, 1)

        def residual(nm, i, down):
            def f(g):
                def q(t):
                    m = HS[nm][0] + 16 * i + 4 * (g - down) + t
                    act.wait_ge(h_sum, m + 1)
                    act.activation(tt[:, t, :], h[:, 4 * (g - down) + t, :], ACT.Square).then_inc(sq_done, 1)
                return q
            return f

        def high(nm, i, m):
            act.wait_ge(r_done, AI[nm] + 16 * i + m + 1)
            act.activation(act_in[:, m, 0:T], tt[:, m % 4, :], ACT.Copy).then_inc(ah_done, 1)

        def run(nm, evac):
            lin = L[nm]
            schedule(loop, lin.iters, lin.lens, split(lin), lambda i, g, t: evac(lin, i, g, t))

        act.wait_ge(h_in, 64)
        squares(h, 0)
        act.wait_ge(par_in, 16)
        act.wait_ge(cols_zero, 2)
        act.activation(silu_c[:, :], col("c", 0, DC), ACT.Silu).then_inc(silu_done, 1)
        norm("mix")
        prepare("mix")
        run("w_in", half)
        mixer["scalar"](act)
        act.wait_ge(mixer["lo"], mixer["lo_all"])

        act.dma_start(memx[:, :, :], A["memT"]).then_inc(mem_in, 16)
        act.wait_ge(mem_in, 16)
        squares(memx, SQ["mem"][0])
        norm("mem")
        prepare("mem")
        run("mix_out", lambda lin, i, g, t: staged(t, lambda t: half(lin, i, g, t), residual("mix_out", i, 0)(g)))
        run("kv", half)
        norm("cross")
        prepare("cross")
        run("q", half)
        cross_scalar(act)
        run("o", lambda lin, i, g, t: staged(t, lambda t: half(lin, i, g, t), residual("o", i, 0)(g)))
        norm("mlp")
        prepare("mlp")

        def mlp(lin, i, g, t):
            if g < 4:
                staged(t, lambda t: half(lin, i, g, t), lambda t: high("mlp", i, 4 * g + t))
            else:
                staged(t, lambda t: half(lin, i, g, t), residual("mlp", i, 4)(g))
        run("mlp", mlp)
        norm("final")
        for j in range(DC):
            act.wait_ge(h_normed, j + 1)
            act.wait_ge(ss_done, SQ["g0"][0] + j - 3)
            act.activation(tt[:, j % 4, :], h[:, j, :], ACT.Square).then_inc(sq_done, 1)
        norm("g0")
        act.wait_ge(mod_done, 3)
        act.dma_start(wst[:, :, :], A["wsT"]).then_inc(mix_in, 16)
        act.dma_start(bsb[:, :, :], A["bsb"]).then_inc(mix_in, 16)
        prepare("g0", 0)

        def a_v(lin, i, g, t):
            def gelu(t):
                m = 8 * i + 4 * g + t
                act.wait_ge(evac_done, lin.tile(i, g, t) + 9)
                apart(act)
                act.activation(one(vmix[:, bass.ds(m, 1), :]), tt[:, t, :], ACT.Gelu_apprx_tanh).then_inc(v_done, 1)
                act.wait_ge(v_done, m + 1)
                apart(act)
                act.activation(tt[:, t, :], one(vmix[:, bass.ds(m, 1), :]), ACT.Square).then_inc(sq_done, 1)
            staged(t, lambda t: half(lin, i, g, t), gelu)
        run("a_v", a_v)
        norm("av")
        mixing_scalar(act)

        def a_uo(lin, i, g, t):
            def gelu(t):
                act.wait_ge(evac_done, lin.tile(i, g, t) + 9)
                act.activation(tt[:, t, :], tt[:, t, :], ACT.Gelu_apprx_tanh).then_inc(g_done, 1)
            if g < 4:
                staged(t, lambda t: half(lin, i, g, t), gelu, lambda t: high("a_uo", i, 4 * g + t))
            else:
                staged(t, lambda t: half(lin, i, g, t), residual("a_uo", i, 4)(g))
        run("a_uo", a_uo)
        norm("g1")
        prepare("g1", 48)

        def ffn(nm, up):
            def f(lin, i, g, t):
                if g >= up:
                    return staged(t, lambda t: half(lin, i, g, t), residual(nm, i, up)(g))
                k4 = FT[nm] + 4 * (len(lin.lens) - 4) * i + 4 * g

                def middle(t):
                    act.wait_ge(evac_done, lin.tile(i, g, t) + 9)
                    apart(act)
                    a = FC[nm] + 16 * i + 2 * g + t % 2
                    c = COL["conv"] + 8 * a + 4 * (t // 2)
                    w = lambda q: par[:, c + q:c + q + 1] if isinstance(c, int) else par[:, bass.ds(c + q, 1)]
                    act.activation(yc[:, t, :], zc[:, t, 1:T + 1], ACT.Identity, bias=w(3), scale=w(1))\
                       .then_inc(y_done, 1)

                def gate(t):
                    if t < 2:
                        act.wait_ge(y_sum, 2 * (k4 + t) + 2)
                        act.activation(yc[:, t, :], yc[:, t, :], ACT.Silu).then_inc(s_done, 1)

                def hi(t):
                    if t >= 2:
                        high(nm, i, 2 * g + t - 2)
                staged(t, lambda t: half(lin, i, g, t), middle, gate, hi)
            return f
        run("ffn", ffn("ffn", 8))
        run("ffn_tail", ffn("ffn_tail", 6))
        norm("out")

    @block.vector
    def _(dve):
        dve.sem_inc(lo_done, RING)
        dve.sem_inc(evac_done, 8)
        dve.sem_inc(ada_sum, 3)
        loop = looped(dve)

        def split(lin, ada_at=None):
            def f(i, p):
                r = p % RING
                n = lin.slot(i, p)
                dve.wait_ge(hi_done, n + 1)
                dve.tensor_tensor(wlo[:, r, :], raw[:, r, :], whi[:, r, :].bitcast(F32), ALU.subtract)\
                   .then_inc(lo_done, 1)
                if ada_at and (ada_at[1] == 4 or p % 2):
                    sum_ada(lin, i, *ada_at, p if ada_at[1] == 4 else p // 2)
            return f

        def sum_ada(lin, i, a0, per, m):
            more = lin.S * per // 4
            n = a0 + i * more + m
            a = a0 // 8 + i * (more // 8) + m // 8
            dve.wait_ge(ada_landed[m % 2], 8 * a0 + i * (8 * more) + 16 * (m // 2) + 16)
            for c in range(2):
                dst = ada[:, a, :] if isinstance(a, int) else one(ada[:, bass.ds(a, 1), :])
                w = adaw[:, m % 2, c * 512:(c + 1) * 512]
                s = silu_c[:, 2 * (m % 8) + c:2 * (m % 8) + c + 1]
                if m % 8 == 0 and c == 0:
                    ins = dve.tensor_scalar(dst, w, s, None, ALU.mult)
                else:
                    dve.wait_ge(ada_sum, 2 * n + c + 3)
                    ins = dve.scalar_tensor_tensor(dst, w, s, dst, ALU.mult, ALU.add)
                ins.then_inc(ada_sum, 1)

        def add(lin, i, g, t, dst):
            dve.wait_ge(hl_done, lin.tile(i, g, t) + 1)
            dve.tensor_tensor(dst, ps[:, lin.bank(g, t), 0:T], hl[:, t, :], ALU.add).then_inc(evac_done, 1)

        def norm(nm, eps, width=D):
            dve.wait_ge(stat_done, NORM[nm] + 1)
            b = stat_bank[nm]
            dve.tensor_scalar(rstd[:, :], ps[:, b, 0:T], 1.0 / width, eps, ALU.mult, ALU.add).then_inc(rt_done, 1)
            dve.wait_ge(rs_done, NORM[nm] + 1)
            dve.reciprocal(rstd[:, :], rstd[:, :]).then_inc(rstd_done, 1)
            dve.wait_ge(rstd_done, NORM[nm] + 1)

        def prepare(nm, src, gain, shift=None):
            def low(j):
                dve.wait_ge(xh_done, XP[nm] + j + 1)
                s = zero[:, :] if shift is None else mod[:, shift + j:shift + j + 1]
                dve.scalar_tensor_tensor(xn[:, j, T:2 * T], tt[:, j % 4, :], s, xn[:, j, 0:T].bitcast(F32),
                                         ALU.add, ALU.subtract).then_inc(xn_ready, 1)
            for j in range(DC):
                dve.scalar_tensor_tensor(tt[:, j % 4, :], src[:, j, :], gain(j), rstd[:, :], ALU.mult, ALU.mult)\
                   .then_inc(xp_done, 1)
                if j:
                    low(j - 1)
            low(DC - 1)

        def residual(nm, i, down, gate=None):
            def f(g):
                def q(t):
                    m = 4 * (g - down) + t
                    dve.wait_ge(ss_done, SQ_AT[nm] + 16 * i + m - 3)
                    add(L[nm], i, g, t, tt[:, t, :])
                    dve.wait_ge(evac_done, L[nm].tile(i, g, t) + 9)
                    if gate is None:
                        ins = dve.tensor_tensor(h[:, m, :], h[:, m, :], tt[:, t, :], ALU.add)
                    else:
                        ins = dve.scalar_tensor_tensor(h[:, m, :], tt[:, t, :], mod[:, gate + m:gate + m + 1],
                                                       h[:, m, :], ALU.mult, ALU.add)
                    ins.then_inc(h_sum, 1)
                return q
            return f

        def low(nm, i, m):
            dve.wait_ge(ah_done, AI[nm] + 16 * i + m + 1)
            dve.tensor_tensor(act_in[:, m, T:2 * T], tt[:, m % 4, :], act_in[:, m, 0:T].bitcast(F32), ALU.subtract)\
               .then_inc(ai_ready, 1)

        def run(nm, evac, ada_at=None):
            lin = L[nm]
            schedule(loop, lin.iters, lin.lens, split(lin, ada_at), lambda i, g, t: evac(lin, i, g, t))

        dve.wait_ge(h_in, 64)
        dve.wait_ge(par_in, 16)
        norm("mix", EPS_1)
        prepare("mix", h, lambda j: col("norm_mix", j))
        dve.wait_ge(silu_done, 1)
        dve.wait_ge(cols_zero, 2)

        run("w_in", lambda lin, i, g, t: add(lin, i, g, t, one(proj[:, bass.ds(8 * i + 4 * g + t, 1), 1:TW])
                                             if not isinstance(i, int) else proj[:, 8 * i + 4 * g + t, 1:TW]))
        mixer["vector"](dve)

        dve.wait_ge(mem_in, 16)
        norm("mem", EPS_1)
        prepare("mem", memx, lambda j: col("norm_mem", j))
        run("mix_out", lambda lin, i, g, t: residual("mix_out", i, 0)(g)(t), ADA_AT["mix_out"])
        run("kv", lambda lin, i, g, t: add(lin, i, g, t, kv[:, 4 * g + t, :]), ADA_AT["kv"])
        norm("cross", EPS_1)
        prepare("cross", h, lambda j: col("norm_cross", j))
        run("q", lambda lin, i, g, t: add(lin, i, g, t, qx[:, t, :]), ADA_AT["q"])
        dve.wait_ge(evac_done, 8 + 4 * L["o"].g0)
        cross_vector(dve)
        run("o", lambda lin, i, g, t: residual("o", i, 0)(g)(t), ADA_AT["o"])
        norm("mlp", EPS_1)
        prepare("mlp", h, lambda j: col("norm_mlp", j))

        def mlp(lin, i, g, t):
            def up(t):
                m = 4 * g + t
                dve.wait_ge(ss_done, SQ_AT["mlp"] + 16 * i)
                add(lin, i, g, t, tt[:, t, :])
                dve.wait_ge(evac_done, lin.tile(i, g, t) + 9)
                dve.scalar_tensor_tensor(tt[:, t, :], tt[:, t, :], 0.0, tt[:, t, :], ALU.max, ALU.mult)\
                   .then_inc(r_done, 1)
            if g < 4:
                staged(t, up, lambda t: low("mlp", i, 4 * g + t))
            else:
                residual("mlp", i, 4)(g)(t)
        run("mlp", mlp, ADA_AT["mlp"])
        norm("final", EPS_1)
        for j in range(DC):
            dve.scalar_tensor_tensor(h[:, j, :], h[:, j, :], col("norm_final", j), rstd[:, :], ALU.mult, ALU.mult)\
               .then_inc(h_normed, 1)
        dve.wait_ge(ada_red, 1)
        dve.tensor_tensor(mod[:, 0:96], ps[:, ada_bank, 0:96], col("ada_b", 0, 96), ALU.add).then_inc(mod_done, 1)
        dve.wait_ge(mod_done, 1)
        for q, nm in ((16, "norm_g0"), (64, "norm_g1")):
            dst = 96 if q == 16 else 96 + DC
            dve.scalar_tensor_tensor(mod[:, dst:dst + DC], mod[:, q:q + DC], 1.0, col(nm, 0, DC), ALU.add, ALU.mult)\
               .then_inc(mod_done, 1)
        norm("g0", EPS_2)
        dve.wait_ge(mod_done, 3)
        prepare("g0", h, lambda j: mod[:, 96 + j:97 + j], 0)

        def a_v(lin, i, g, t):
            dve.wait_ge(ss_done, SQ["av"][0] + 8 * i + 4 * g + t - 3)
            add(lin, i, g, t, tt[:, t, :])
        run("a_v", a_v)
        norm("av", EPS_2, 4096)
        dve.wait_ge(v_done, 32)
        dve.wait_ge(mix_in, 32)
        mixing_vector(dve)
        for r in range(2):
            MD.wait(dve, r, 7, "s1")

        def a_uo(lin, i, g, t):
            def u(t):
                dve.wait_ge(ss_done, SQ_AT["a_uo"] + 16 * i)
                add(lin, i, g, t, tt[:, t, :])

            def times_s(t):
                m = 4 * g + t
                dve.wait_ge(g_done, 16 * i + m + 1)
                v = vmix[:, 16 * i + m, :] if isinstance(i, int) else one(vmix[:, bass.ds(16 * i + m, 1), :])
                dve.tensor_tensor(tt[:, t, :], tt[:, t, :], v, ALU.mult).then_inc(r_done, 1)
            if g < 4:
                staged(t, u, times_s, lambda t: low("a_uo", i, 4 * g + t))
            else:
                residual("a_uo", i, 4, 32)(g)(t)
        run("a_uo", a_uo)
        norm("g1", EPS_2)
        prepare("g1", h, lambda j: mod[:, 96 + DC + j:97 + DC + j], 48)
        dve.memset(zc[:, :, 0:1], 0.0).then_inc(pads, 1)
        dve.memset(zc[:, :, T + 1:T + 2], 0.0).then_inc(pads, 1)
        dve.wait_ge(pads, 2)

        def ffn(nm, up):
            def f(lin, i, g, t):
                if g >= up:
                    return residual(nm, i, up, 80)(g)(t)
                k4 = FT[nm] + 4 * (len(lin.lens) - 4) * i + 4 * g

                def z(t):
                    add(lin, i, g, t, zc[:, t, 1:T + 1])

                def taps(t):
                    a = FC[nm] + 16 * i + 2 * g + t % 2
                    c = COL["conv"] + 8 * a + 4 * (t // 2)
                    w = lambda q: par[:, c + q:c + q + 1] if isinstance(c, int) else par[:, bass.ds(c + q, 1)]
                    dve.wait_ge(y_done, k4 + t + 1)
                    dve.scalar_tensor_tensor(yc[:, t, :], zc[:, t, 0:T], w(0), yc[:, t, :], ALU.mult, ALU.add)\
                       .then_inc(y_sum, 1)
                    dve.wait_ge(y_sum, 2 * (k4 + t) + 1)
                    dve.scalar_tensor_tensor(yc[:, t, :], zc[:, t, 2:T + 2], w(2), yc[:, t, :], ALU.mult, ALU.add)\
                       .then_inc(y_sum, 1)

                def product(t):
                    if t >= 2:
                        m = 2 * g + t - 2
                        dve.wait_ge(ss_done, SQ_AT[nm] + 16 * i)
                        dve.wait_ge(s_done, (2 * (len(lin.lens) - 4) * i + FT[nm] // 2) + 2 * g + t - 1)
                        dve.wait_ge(y_sum, 2 * (k4 + t) + 2)
                        dve.tensor_tensor(tt[:, m % 4, :], yc[:, t - 2, :], yc[:, t, :], ALU.mult).then_inc(r_done, 1)

                def lo(t):
                    if t >= 2:
                        low(nm, i, 2 * g + t - 2)
                staged(t, z, taps, product, lo)
            return f
        run("ffn", ffn("ffn", 8))
        run("ffn_tail", ffn("ffn_tail", 6))
        norm("out", EPS_2)
        for j in range(DC):
            dve.scalar_tensor_tensor(fin[:, j, :], h[:, j, :], col("final_g", j), rstd[:, :], ALU.mult, ALU.mult)\
               .then_inc(fin_done, 1)

    @block.tensor
    def _(pe):
        pe.sem_inc(slot_used, RING)

        def group(lin, i, g, x, ready):
            p0 = lin.ends[g] - lin.lens[g]
            for s in range(lin.lens[g]):
                r = (p0 + s) % RING
                pe.wait_ge(lo_done, lin.slot(i, p0 + s) + 1 + RING)
                for c in range(2):
                    kc = 2 * s + c
                    first, last = kc == 0, kc == 2 * lin.lens[g] - 1
                    if ready:
                        pe.wait_ge(ready[0], ready[1] + kc + 1)
                    for t in range(4):
                        if first:
                            pe.wait_ge(evac_done, lin.tile(i, g, t) + 1)
                        b = lin.bank(g, t)
                        w = slice(c * 512 + t * P, c * 512 + (t + 1) * P)
                        if not last:
                            pe.matmul(ps[:, b, :], whi[:, r, w], x[:, kc, :], start=first, stop=False)
                        ins = pe.matmul(ps[:, b, 0:T], wlo[:, r, w], x[:, kc, 0:T], start=False, stop=False)
                        if last:
                            ins = pe.matmul(ps[:, b, :], whi[:, r, w], x[:, kc, :], start=False, stop=True)
                            if t < 3:
                                ins.then_inc(tile_done, 1)
                ins.then_inc(slot_used, 1)

        def run(nm, x, ready):
            lin = L[nm]

            def body(i, _):
                for g in range(len(lin.lens)):
                    xx, rd = (x(g), ready(i, g)) if callable(x) else (x, ready)
                    group(lin, i, g, xx, rd)
            if lin.iters > 1:
                with pe.Fori(0, lin.iters) as i:
                    body(i, False)
            else:
                body(0, True)

        def stat(nm, after=None):
            b = stat_bank[nm]
            pe.wait_ge(ss_done, SQ[nm][1])
            if after is not None:
                pe.wait_ge(evac_done, 4 * after + 1)
            pe.matmul(ps[:, b, 0:T], ones[:, :], ss[:, :], start=True, stop=True).then_inc(stat_done, 1)

        pe.wait_ge(const_in, 32)
        stat("mix")
        run("w_in", xn, (xn_ready, XP["mix"]))
        mixer["tensor"](pe)
        pe.wait_ge(mixer["lo"], mixer["lo_all"])
        stat("mem")
        run("mix_out", act_in, None)
        run("kv", xn, (xn_ready, XP["mem"]))
        stat("cross", L["q"].g0)
        run("q", xn, (xn_ready, XP["cross"]))
        pe.wait_ge(evac_done, 8 + 4 * L["o"].g0)
        cross_tensor(pe)
        XD.wait(pe, 0, 0, "lo3")
        run("o", act_in, None)
        stat("mlp", L["mlp"].g0)
        run("mlp", lambda g: xn if g < 4 else act_in,
            lambda i, g: {0: (xn_ready, XP["mlp"]), 4: (ai_ready, AI["mlp"] + 16 * i)}.get(g))
        stat("final", L["a_v"].g0)
        pe.wait_ge(ada_sum, 3 + 2 * 192)
        pe.wait_ge(evac_done, 8 + 4 * L["a_v"].g0)
        for a in range(24):
            for t in range(4):
                ins = pe.matmul(ps[:, ada_bank, 4 * a + t:4 * a + t + 1], ada[:, a, t * P:(t + 1) * P], ones[:, 0:1],
                                start=True, stop=True)
        ins.then_inc(ada_red, 1)
        pe.wait_ge(rt_done, NORM["final"] + 1)
        stat("g0")
        run("a_v", xn, (xn_ready, XP["g0"]))
        stat("av", L["a_uo"].g0)
        pe.wait_ge(mix_in, 32)
        pe.wait_ge(evac_done, 8 + 4 * L["a_uo"].g0)
        mixing_tensor(pe)
        for r in range(2):
            MD.wait(pe, r, 7, "s1")
        run("a_uo", lambda g: xn if g < 4 else act_in,
            lambda i, g: {4: (ai_ready, AI["a_uo"] + 16 * i)}.get(g))
        stat("g1", L["ffn"].g0)
        run("ffn", lambda g: xn if g < 8 else act_in,
            lambda i, g: {0: (xn_ready, XP["g1"]), 8: (ai_ready, AI["ffn"] + 16 * i)}.get(g))
        run("ffn_tail", lambda g: xn if g < 6 else act_in,
            lambda i, g: {6: (ai_ready, AI["ffn_tail"])}.get(g))
        stat("out", L["ffn_tail"].g0 + 10)

    ctx.close()


def _chunks(v):
    return np.asarray(v, np.float32).reshape(-1, P).T


def _slots(w, groups):
    rows = w.shape[0]
    outs = []
    for cols in groups:
        parts = [w[:, a:b] if b > a else np.zeros((rows, a - b), w.dtype) for a, b in cols]
        g = np.concatenate(parts, 1) if len(parts) > 1 else parts[0]
        assert g.shape[1] == 512, g.shape
        outs.append(g.reshape(rows // 256, 2, P, 512).transpose(0, 2, 1, 3).reshape(rows // 256, P, SLOT))
    return outs


def _plain(w, c0=0, n=None, r0=0, r1=None):
    n = w.shape[1] if n is None else n
    return _slots(w[r0:r1], [[(c, c + 512)] for c in range(c0, c0 + n, 512)])


def _arrays(x):
    f = {k: np.asarray(v) for k, v in x.items()}
    w_in = f["w_in"][0]
    lo = 3072
    z = lambda n: (n, 0)
    groups = [[(512 * g, 512 * g + 512)] for g in range(6)]
    groups += [[(3360 + 512 * g, 3872 + 512 * g)] for g in range(5)]
    groups += [[(lo, lo + 128), (lo + 128, lo + 256), (lo + 256, lo + 288), z(96), (5920, 6000), z(48)]]
    s = _slots(w_in, groups)
    s += _plain(f["w_mix_out"][0])
    s += _plain(f["w_kv_cross"][0])
    s += _plain(f["w_q_cross"][0])
    s += _plain(f["w_o_cross"][0])
    up, down = f["w_up"][0], f["w_down"][0]
    for q in range(4):
        s += _plain(up, D * q, D)
        s += _plain(down, r0=D * q, r1=D * q + D)
    a_in, a_out = f["a_w_in_2"][0], f["a_w_out_2"][0]
    s += _plain(a_in, 4096, 4096)
    for q in range(2):
        s += _plain(a_in, D * q, D)
        s += _plain(a_out, r0=D * q, r1=D * q + D)
    fu, fd = f["ffn_w_up_2"][0], f["ffn_w_down_2"][0]
    for a, b in ((0, 2048), (2048, 4096), (4096, FF2)):
        s += _slots(fu, [[(c, c + 256), (FF2 + c, FF2 + c + 256)] for c in range(a, b, 256)])
        s += _plain(fd, r0=a, r1=b)
    stream = np.concatenate(s, 0)
    ada = np.concatenate(_plain(f["ada_w_2"][0]), 0)

    par = np.zeros((P, NPAR), np.float32)

    def put(name, v, j=0):
        par[:, COL[name] + j:COL[name] + j + v.shape[1]] = v

    for name, key in [("norm_mix", "norm_mix"), ("norm_cross", "norm_cross"), ("norm_mem", "norm_mem"),
                      ("norm_mlp", "norm_mlp"), ("w0", "w_decay0"), ("a0", "a0"), ("k_k", "k_k"), ("k_a", "k_a"),
                      ("lnx_w", "lnx_w"), ("lnx_b", "lnx_b"), ("ada_b", "ada_b_2"), ("g_v", "a_g_v_2")]:
        put(name, _chunks(f[key][0]))
    put("r_k", _chunks(f["r_k"][0].reshape(-1)))
    put("norm_final", _chunks(f["norm_final"]))
    put("norm_g0", _chunks(f["norm_g_2"][0, 0]))
    put("norm_g1", _chunks(f["norm_g_2"][0, 1]))
    put("final_g", _chunks(f["final_g_2"]))
    put("c", _chunks(f["c_2"][0]))
    mu = f["rwkv_mu"][0]
    put("mu", _chunks(mu[:3328]))
    par[0:32, COL["mu"] + 26] = mu[3328:3360]
    cw, cb = f["ffn_conv_w_2"][0], f["ffn_conv_b_2"][0]
    conv = np.stack([*cw, cb]).reshape(4, 2, FF2C, P)
    put("conv", conv.transpose(3, 2, 1, 0).reshape(P, FF2C * 8))
    for q, (width, half) in enumerate(((128, 16), (64, 8))):
        inv = (np.float32(THETA) ** (-np.arange(half, dtype=np.float32) / np.float32(half))).astype(np.float32)
        p = np.arange(P) % width
        par[:, COL["inv_freq"] + q] = np.where(p < 2 * half, inv[p % half], 0)
    par[np.arange(P), COL["i64"] + np.arange(P) % CH] = 1

    i = np.arange(P)
    const = np.zeros((P, 8, P), np.float32)
    const[:, C_ID] = np.eye(P)
    const[:, C_ONES] = 1
    same = i[:, None] // CH == i[None, :] // CH
    const[:, C_BLK1] = same
    const[:, C_BLK64] = same / CH
    for m in range(16):
        const[m + 16, C_ROPE, m], const[m, C_ROPE, m + 16] = -1, 1
    for hd in range(2):
        for m in range(8):
            const[64 * hd + m + 8, C_ROPEI, 64 * hd + m], const[64 * hd + m, C_ROPEI, 64 * hd + m + 8] = -1, 1
            const[m + 8, C_DUPR, 64 * hd + m], const[m, C_DUPR, 64 * hd + m + 8] = -1, 1
        for m in range(64):
            const[m, C_DUP, 64 * hd + m] = 1
    masks = np.zeros((P, 12, P), np.float32)
    s_, t_ = i[:, None], i[None, :]
    masks[:, 0] = masks[:, 2] = same & (s_ < t_)
    masks[:, 1] = masks[:, 3] = same & (s_ <= t_)
    for lv in range(6):
        b = 2 ** lv
        masks[:, 4 + lv] = (s_ // (2 * b) == t_ // (2 * b)) & (t_ // b % 2 == 1) & (s_ // b % 2 == 0)
    masks[:, 10:12] = (np.arange(T) % CH != 0).reshape(2, P)
    lora = np.zeros((RWT, P, 4, P), np.float32)
    tiles = lambda w: w.reshape(w.shape[0], RWT, P).transpose(1, 0, 2)
    lora[:, 0:64, 0] = tiles(f["w_decay_up"][0])
    lora[:, 64:128, 1] = tiles(f["a_up"][0])
    lora[:, :, 2] = tiles(f["g_up"][0][0:128])
    lora[:, 0:32, 3] = tiles(f["g_up"][0][128:160])
    feat = lambda v: np.ascontiguousarray(v.T.reshape(DC, P, T).transpose(1, 0, 2))
    return {
        "xT": feat(f["x"][0]), "memT": feat(f["mem"][0]), "pos": f["positions"].astype(np.int32), "stream": stream,
        "ada": ada, "par": par, "const": const, "masks": masks, "lora": lora,
        "wsT": np.ascontiguousarray(f["a_w_s_2"][0].transpose(2, 0, 1)),
        "bsb": np.ascontiguousarray(np.broadcast_to(f["a_b_s_2"][0][None], (P, 16, P))),
    }


def kernel(**inputs):
    import concourse.bacc as bacc
    from concourse.bass_utils import run_bass_kernel_spmd

    nc = bacc.Bacc("TRN2", target_bir_lowering=False, num_devices=1)
    arrays = _arrays(inputs)
    A = {k: nc.dram_tensor(f"in_{k}", v.shape, mybir.dt.from_np(v.dtype), kind="ExternalInput").ap()
         for k, v in arrays.items()}
    out = nc.dram_tensor("out", (P, DC, T), F32, kind="ExternalOutput").ap()
    build(nc, A, out)
    r = run_bass_kernel_spmd(nc, [{f"in_{k}": v for k, v in arrays.items()}], core_ids=[0])
    got = r.results[0]["out"]
    return np.ascontiguousarray(got.transpose(1, 0, 2).reshape(D, T).T)[None]
```
